# Optimizing a Trainium2 kernel written in Bass

```python
import jax, jax.numpy as jnp
from jax import lax
import numpy as np

D_MODEL = 1024
BATCH = 1
SEQ = 1024
DEPTH = 1

HEAD_DIM = 64
RET_HEADS = 8
NSA_Q_HEADS = 8
NSA_KV_HEADS = 2
NSA_GROUP = NSA_Q_HEADS // NSA_KV_HEADS
RET_WIDTH = RET_HEADS * HEAD_DIM
NSA_WIDTH = NSA_Q_HEADS * HEAD_DIM
MIX_WIDTH = RET_WIDTH + NSA_WIDTH
KV_WIDTH = NSA_KV_HEADS * HEAD_DIM
RET_CHUNK = 128
RET_THETA = 10000.0
ROPE_THETA = 500000.0
ROPE_DIM = HEAD_DIM // 4
CMP_BLOCK = 32
CMP_STRIDE = 16
CMP_HIDDEN = 256
SEL_BLOCK = 64
SEL_TOPK = 16
WINDOW = 512
NSA_QBLOCK = 64
N_BRANCH = 3
D_FF = 2816
CONV_WIDTH = 3
PLE_DIM = 256
EPS = 1e-6

IN_SIZES = [RET_WIDTH, RET_WIDTH, RET_WIDTH, RET_WIDTH,
            NSA_WIDTH,
            KV_WIDTH, KV_WIDTH, KV_WIDTH, KV_WIDTH, KV_WIDTH, KV_WIDTH,
            NSA_Q_HEADS * N_BRANCH]
IN_WIDTH = int(sum(IN_SIZES))
IN_SPLITS = [int(v) for v in np.cumsum(IN_SIZES)[:-1]]

kernel_name = 'hymba_retnet_nsa_convffn_ple'

def rms_norm(x, w):
    x32 = x.astype(jnp.float32)
    y = x32 * lax.rsqrt(jnp.mean(x32 * x32, axis=-1, keepdims=True) + EPS)
    return (y * w.astype(jnp.float32)).astype(x.dtype)

def rope(x, pos, rot_dim, theta):
    half = rot_dim // 2
    inv = jnp.power(jnp.float32(theta), -jnp.arange(half, dtype=jnp.float32) / half)
    ang = pos.astype(jnp.float32)[..., None] * inv
    cos = jnp.cos(ang)[:, :, None, :].astype(x.dtype)
    sin = jnp.sin(ang)[:, :, None, :].astype(x.dtype)
    x1, x2, rest = x[..., :half], x[..., half:rot_dim], x[..., rot_dim:]
    return jnp.concatenate([x1 * cos - x2 * sin, x1 * sin + x2 * cos, rest], axis=-1)

def masked_softmax(s, mask):
    s = jnp.where(mask, s.astype(jnp.float32), -jnp.inf)
    m = jnp.max(s, axis=-1, keepdims=True)
    m = jnp.where(jnp.isfinite(m), m, 0.0)
    e = jnp.exp(s - m)
    return e / jnp.maximum(jnp.sum(e, axis=-1, keepdims=True), 1e-30)

def retention(q, k, v):
    B, S, H, d = q.shape
    C = RET_CHUNK
    NC = S // C
    dt = q.dtype
    log_g = jnp.log1p(-jnp.exp2(-5.0 - jnp.arange(H, dtype=jnp.float32)))
    pos = jnp.arange(C, dtype=jnp.float32)
    diff = pos[:, None] - pos[None, :]
    decay = jnp.where(diff >= 0, jnp.exp(jnp.maximum(diff, 0.0) * log_g[:, None, None]), 0.0).astype(dt)
    q_decay = jnp.exp((pos + 1.0) * log_g[:, None]).astype(dt).T
    k_decay = jnp.exp((C - 1.0 - pos) * log_g[:, None]).astype(dt).T
    chunk_decay = jnp.exp(C * log_g).astype(dt)
    qc = q.reshape(B, NC, C, H, d)
    kc = k.reshape(B, NC, C, H, d)
    vc = v.reshape(B, NC, C, H, d)
    scores = jnp.einsum('bnchd,bnkhd->bhnck', qc, kc) * decay[None, :, None]
    o_intra = jnp.einsum('bhnck,bnkhd->bnchd', scores, vc)
    kv = jnp.einsum('bnkhd,bnkhe->nbhde', kc * k_decay[None, None, :, :, None], vc)

    def step(state, kv_n):
        return state * chunk_decay[None, :, None, None] + kv_n, state

    _, prev = lax.scan(step, jnp.zeros_like(kv[0]), kv)
    o_cross = jnp.einsum('bnchd,nbhde->bnche', qc * q_decay[None, None, :, :, None], prev)
    return (o_intra + o_cross).reshape(B, S, H, d)

def nsa(q, k_cmp, v_cmp, k_slc, v_slc, k_win, v_win, gates,
        cmp_pos, cmp_k_w1, cmp_k_w2, cmp_v_w1, cmp_v_w2):
    B, S, Hq, d = q.shape
    G, R = NSA_KV_HEADS, NSA_GROUP
    dt = q.dtype
    scale = d ** -0.5
    n_cmp = (S - CMP_BLOCK) // CMP_STRIDE + 1
    tok = jnp.arange(n_cmp)[:, None] * CMP_STRIDE + jnp.arange(CMP_BLOCK)[None, :]

    def compress(t, w1, w2):
        blocks = t[:, tok] + cmp_pos[:, None, :]
        flat = blocks.transpose(0, 3, 1, 2, 4).reshape(B, G, n_cmp, CMP_BLOCK * d)
        return jax.nn.gelu(flat @ w1) @ w2

    ck = compress(k_cmp, cmp_k_w1, cmp_k_w2)
    cv = compress(v_cmp, cmp_v_w1, cmp_v_w2)
    ci = jnp.arange(n_cmp)
    cmp_end = ci * CMP_STRIDE + CMP_BLOCK - 1
    n_sel = S // SEL_BLOCK
    top = min(SEL_TOPK, n_sel)
    ks_blocks = k_slc.transpose(0, 2, 1, 3).reshape(B, G, n_sel, SEL_BLOCK, d)
    vs_blocks = v_slc.transpose(0, 2, 1, 3).reshape(B, G, n_sel, SEL_BLOCK, d)
    sj = jnp.arange(n_sel)
    overlap = ((ci[:, None] * CMP_STRIDE < (sj[None, :] + 1) * SEL_BLOCK)
               & (ci[:, None] * CMP_STRIDE + CMP_BLOCK > sj[None, :] * SEL_BLOCK)).astype(jnp.float32)
    pad = ((0, 0), (0, 0), (WINDOW, 0), (0, 0))
    kw = jnp.pad(k_win.transpose(0, 2, 1, 3), pad)
    vw = jnp.pad(v_win.transpose(0, 2, 1, 3), pad)
    QB = NSA_QBLOCK
    nqb = S // QB
    qb = q.reshape(B, nqb, QB, G, R, d).transpose(1, 0, 3, 4, 2, 5)
    bi = jnp.arange(B)[:, None, None, None]
    gi = jnp.arange(G)[None, :, None, None]

    def block(args):
        qi, i = args
        t0 = i * QB
        t = t0 + jnp.arange(QB)
        s = jnp.einsum('bgrqd,bgnd->bgrqn', qi, ck) * scale
        p_c = masked_softmax(s, cmp_end[None, :] <= t[:, None])
        o_c = jnp.einsum('bgrqn,bgnd->bgrqd', p_c.astype(dt), cv)
        imp = jnp.einsum('bgrqn,ns->bgqs', p_c, overlap)
        cur = t // SEL_BLOCK
        valid = sj[None, :] * SEL_BLOCK <= t[:, None]
        forced = (sj[None, :] == 0) | (sj[None, :] == cur[:, None]) | (sj[None, :] == cur[:, None] - 1)
        score = jnp.where(forced, jnp.inf, jnp.where(valid, imp, -jnp.inf))
        _, idx = lax.top_k(score, top)
        ksel = ks_blocks[bi, gi, idx].reshape(B, G, QB, top * SEL_BLOCK, d)
        vsel = vs_blocks[bi, gi, idx].reshape(B, G, QB, top * SEL_BLOCK, d)
        kpos = (idx[..., None] * SEL_BLOCK + jnp.arange(SEL_BLOCK)).reshape(B, G, QB, top * SEL_BLOCK)
        smask = kpos <= t[:, None]
        s = jnp.einsum('bgrqd,bgqkd->bgrqk', qi, ksel) * scale
        p_s = masked_softmax(s, smask[:, :, None])
        o_s = jnp.einsum('bgrqk,bgqkd->bgrqd', p_s.astype(dt), vsel)
        kwi = lax.dynamic_slice_in_dim(kw, t0, QB + WINDOW, axis=2)
        vwi = lax.dynamic_slice_in_dim(vw, t0, QB + WINDOW, axis=2)
        wpos = t0 - WINDOW + jnp.arange(QB + WINDOW)
        wmask = (wpos[None, :] >= 0) & (wpos[None, :] <= t[:, None]) & (wpos[None, :] > t[:, None] - WINDOW)
        s = jnp.einsum('bgrqd,bgkd->bgrqk', qi, kwi) * scale
        p_w = masked_softmax(s, wmask)
        o_w = jnp.einsum('bgrqk,bgkd->bgrqd', p_w.astype(dt), vwi)
        return o_c, o_s, o_w

    o_c, o_s, o_w = lax.map(block, (qb, jnp.arange(nqb)))
    unblock = lambda o: o.transpose(1, 0, 4, 2, 3, 5).reshape(B, S, Hq, d)
    o = (gates[..., 0:1] * unblock(o_c) + gates[..., 1:2] * unblock(o_s)
         + gates[..., 2:3] * unblock(o_w))
    return o.reshape(B, S, Hq * d)

def causal_dwconv(u, w, b):
    K = w.shape[0]
    S = u.shape[1]
    up = jnp.pad(u, ((0, 0), (K - 1, 0), (0, 0)))
    y = b
    for j in range(K):
        y = y + w[j] * up[:, j:j + S]
    return y

def setup_inputs(seed: int = 0) -> dict:
    key = jax.random.key(seed)
    ks = jax.random.split(key, 24)
    nrm = lambda k, shape, s: jax.random.normal(k, shape, jnp.float32) * s
    L = DEPTH
    inp = {}
    inp['x'] = nrm(ks[0], (BATCH, SEQ, D_MODEL), 1.0)
    inp['p'] = nrm(ks[1], (DEPTH, BATCH, SEQ, PLE_DIM), 1.0)
    offset = jax.random.randint(ks[2], (BATCH, 1), 0, 4096, dtype=jnp.int32)
    inp['positions'] = offset + jnp.arange(SEQ, dtype=jnp.int32)[None, :]
    inp['norm_mix_w'] = 1.0 + nrm(ks[3], (L, D_MODEL), 0.02)
    inp['w_in'] = nrm(ks[4], (L, D_MODEL, IN_WIDTH), D_MODEL ** -0.5)
    inp['ret_gn_w'] = 1.0 + nrm(ks[5], (L, RET_WIDTH), 0.02)
    inp['cmp_pos'] = nrm(ks[6], (L, CMP_BLOCK, HEAD_DIM), 0.02)
    inp['cmp_k_w1'] = nrm(ks[7], (L, CMP_BLOCK * HEAD_DIM, CMP_HIDDEN), (CMP_BLOCK * HEAD_DIM) ** -0.5)
    inp['cmp_k_w2'] = nrm(ks[8], (L, CMP_HIDDEN, HEAD_DIM), CMP_HIDDEN ** -0.5)
    inp['cmp_v_w1'] = nrm(ks[9], (L, CMP_BLOCK * HEAD_DIM, CMP_HIDDEN), (CMP_BLOCK * HEAD_DIM) ** -0.5)
    inp['cmp_v_w2'] = nrm(ks[10], (L, CMP_HIDDEN, HEAD_DIM), CMP_HIDDEN ** -0.5)
    inp['w_out'] = nrm(ks[11], (L, MIX_WIDTH, D_MODEL), MIX_WIDTH ** -0.5)
    inp['norm_ffn_w'] = 1.0 + nrm(ks[12], (L, D_MODEL), 0.02)
    inp['ffn_w_up'] = nrm(ks[13], (L, D_MODEL, 2 * D_FF), D_MODEL ** -0.5)
    inp['ffn_conv_w'] = nrm(ks[14], (L, CONV_WIDTH, D_FF), CONV_WIDTH ** -0.5)
    inp['ffn_conv_b'] = nrm(ks[15], (L, D_FF), 0.01)
    inp['ffn_w_down'] = nrm(ks[16], (L, D_FF, D_MODEL), D_FF ** -0.5)
    inp['ple_w'] = nrm(ks[17], (L, PLE_DIM, D_MODEL), PLE_DIM ** -0.5)
    inp['ple_gate_w'] = nrm(ks[18], (L, D_MODEL, D_MODEL), D_MODEL ** -0.5)
    inp['final_norm_w'] = 1.0 + nrm(ks[19], (D_MODEL,), 0.02)
    return inp

def reference(x, p, positions, norm_mix_w, w_in, ret_gn_w, cmp_pos, cmp_k_w1, cmp_k_w2,
              cmp_v_w1, cmp_v_w2, w_out, norm_ffn_w, ffn_w_up, ffn_conv_w, ffn_conv_b,
              ffn_w_down, ple_w, ple_gate_w, final_norm_w):
    B, S, D = x.shape
    h = x
    for i in range(DEPTH):
        xn = rms_norm(h, norm_mix_w[i])
        proj = xn @ w_in[i]
        (rq, rk, rv, rg, nq, kc, vc, ksl, vsl, kwn, vwn, ng) = jnp.split(proj, IN_SPLITS, axis=-1)
        heads = lambda t, n: t.reshape(B, S, n, HEAD_DIM)
        rq = rope(heads(rq, RET_HEADS), positions, HEAD_DIM, RET_THETA)
        rk = rope(heads(rk, RET_HEADS), positions, HEAD_DIM, RET_THETA) * (HEAD_DIM ** -0.5)
        ro = retention(rq, rk, heads(rv, RET_HEADS)).astype(jnp.float32)
        mu = jnp.mean(ro, axis=-1, keepdims=True)
        var = jnp.mean(jnp.square(ro - mu), axis=-1, keepdims=True)
        ro = ((ro - mu) * lax.rsqrt(var + EPS)).reshape(B, S, RET_WIDTH) * ret_gn_w[i].astype(jnp.float32)
        ret_out = ro.astype(h.dtype) * jax.nn.silu(rg)
        prope = lambda t, n: rope(heads(t, n), positions, ROPE_DIM, ROPE_THETA)
        nsa_out = nsa(prope(nq, NSA_Q_HEADS),
                      prope(kc, NSA_KV_HEADS), heads(vc, NSA_KV_HEADS),
                      prope(ksl, NSA_KV_HEADS), heads(vsl, NSA_KV_HEADS),
                      prope(kwn, NSA_KV_HEADS), heads(vwn, NSA_KV_HEADS),
                      jax.nn.sigmoid(ng.reshape(B, S, NSA_Q_HEADS, N_BRANCH)),
                      cmp_pos[i], cmp_k_w1[i], cmp_k_w2[i], cmp_v_w1[i], cmp_v_w2[i])
        h = h + jnp.concatenate([ret_out, nsa_out], axis=-1) @ w_out[i]
        hn = rms_norm(h, norm_ffn_w[i])
        gate_pre, val = jnp.split(hn @ ffn_w_up[i], 2, axis=-1)
        gate = causal_dwconv(gate_pre, ffn_conv_w[i], ffn_conv_b[i])
        h = h + (jax.nn.silu(gate) * val) @ ffn_w_down[i]
        h = h + jax.nn.sigmoid(h @ ple_gate_w[i]) * (p[i] @ ple_w[i])
    return rms_norm(h, final_norm_w)


_drawn_inputs = setup_inputs


def setup_inputs(seed=0):
    import zlib

    import numpy as np

    out = dict(_drawn_inputs(seed))
    spreads = {}
    factors = {'norm_mix_w': 3.512,
     'ret_gn_w': 6.956,
     'cmp_pos': 57.99,
     'norm_ffn_w': 11.945,
     'ffn_conv_b': 32.301,
     'final_norm_w': 22.845,
     'p': 8.0,
     'ple_w': 8.0,
     'ple_gate_w': 8.0}
    for name, (base, spread) in spreads.items():
        noise = np.random.default_rng([zlib.crc32(name.encode()), seed]).standard_normal(out[name].shape)
        drawn = base * np.exp(spread * noise) if base else spread * noise
        out[name] = __import__('jax').numpy.asarray(drawn.astype(out[name].dtype))
    for name, factor in factors.items():
        out[name] = (out[name] * factor).astype(out[name].dtype)
    return out
```

```python
from contextlib import ExitStack

import numpy as np

import concourse.bass as bass
from concourse import mybir

ALU = mybir.AluOpType
ACT = mybir.ActivationFunctionType
AX_X = mybir.AxisListType.X
F32 = mybir.dt.float32
F32R = mybir.dt.float32r
BF16 = mybir.dt.bfloat16
I32 = mybir.dt.int32

P = 128
S = 1024
D = 1024
NT = S // P
NK = D // P
HD = 64
RH = 8
QH = 8
G = 2
RG = QH // G
CMP_BLOCK, CMP_STRIDE, CMP_HID = 32, 16, 256
NCMP = (S - CMP_BLOCK) // CMP_STRIDE + 1
CJ = CMP_BLOCK // 2
WIN_T = 4
FF = 2816
NF = FF // P
PLE = 256
NP_ = PLE // P
EPS = 1e-6
SCALE = HD ** -0.5
MASKED = -1e30
FLOOR = -1e29
CH = 512
CW = [CH] * 6 + [2 * P + 3 * QH]
NCH = len(CW)
ROPE_R, ROPE_N = HD // 2, HD // 8
NA = ROPE_R + ROPE_N
PI_IN = 3.1415925
MAGIC = 1.5 * 2.0 ** 23
DBG = {}

C_ID = 0
C_DIAG = C_ID + P
C_FAR = C_DIAG + P
C_CMP = C_FAR + P
C_DT = C_CMP + NT * HD
C_KD = C_DT + RH * P
C_QD = C_KD + RH
C_CD = C_QD + RH
C_INV = C_CD + RH
C_HALF = C_INV + NA
C_N = C_HALF + NT


def constants():
    c = np.zeros((P, C_N), np.float32)
    p, f = np.arange(P)[:, None], np.arange(P)[None, :]
    c[:, C_ID:C_ID + P] = p == f
    c[:, C_DIAG:C_DIAG + P] = np.where(f <= p, 0.0, MASKED)
    c[:, C_FAR:C_FAR + P] = np.where(f > p, 0.0, MASKED)
    n = np.arange(NCMP)[None, None, :]
    t = np.arange(NT)[None, :, None] * P + np.arange(P)[:, None, None]
    cm = np.zeros((P, NT, HD))
    cm[:, :, :NCMP] = np.where(n * CMP_STRIDE + CMP_BLOCK - 1 <= t, 0.0, MASKED)
    c[:, C_CMP:C_CMP + NT * HD] = cm.reshape(P, -1)
    log_g = np.log1p(-np.exp2(-5.0 - np.arange(RH)))
    for h in range(RH):
        c[:, C_DT + h * P:C_DT + (h + 1) * P] = np.where(f >= p, np.exp(np.maximum(f - p, 0) * log_g[h]), 0.0)
        c[:, C_KD + h] = np.exp((P - 1.0 - np.arange(P)) * log_g[h])
        c[:, C_QD + h] = np.exp((np.arange(P) + 1.0) * log_g[h])
        c[:, C_CD + h] = np.exp(P * log_g[h])
    for at, half, theta in ((0, ROPE_R, 10000.0), (ROPE_R, ROPE_N, 500000.0)):
        e = -np.arange(half, dtype=np.float32) / np.float32(half)
        c[:, C_INV + at:C_INV + at + half] = np.power(np.float32(theta), e)
    c[:, C_HALF:] = -0.5
    return c


def two_pi_parts():
    rest, parts = 2 * np.pi, []
    for _ in range(3):
        m = 2.0 ** (np.floor(np.log2(rest)) - 7)
        parts.append(float(np.floor(rest / m) * m))
        rest -= parts[-1]
    return parts + [float(np.float32(rest))]


class Region:

    def __init__(self, nc, at):
        self.nc, self.at = nc, at

    def put(self, name, shape, dt):
        size = {BF16: 2}.get(dt, 4) * int(np.prod(shape[1:]))
        t = self.nc.alloc_sbuf_tensor_at(name, shape, dt, offset=self.at)
        self.at += (size + 31) // 32 * 32
        return t


def build(nc, xt, x, pt, pos, cst_d, wmix_d, wffn_d, gnw, w_in, cpos, ck_w1, ck_w2, cv_w1, cv_w2,
          w_out, w_up, conv_d, w_down, ple_w, ple_gw, fnw, out):
    proj_d = nc.dram_tensor("proj_d", [S, 6 * CH + 2 * P], F32, **DBG).ap()
    reto_d = nc.dram_tensor("reto_d", [S, RH * HD], F32, **DBG).ap()

    ctx = ExitStack()
    with ctx:
        def sem(name):
            return ctx.enter_context(nc.semaphore(name))

        def sems(name, n):
            return [sem(f"{name}{i}") for i in range(n)]

        ps = ctx.enter_context(nc.psum_tensor("ps", [P, 8, 512], F32))

        base = Region(nc, 16512)
        cst = base.put("cst", [P, C_N], F32)
        ident_r = base.put("ident_r", [P, P], F32R)
        ident_b = base.put("ident_b", [P, P], BF16)
        masks_b = base.put("masks_b", [P, 2 * P + NT * HD], BF16)
        wmix = base.put("wmix", [P, NK], F32)
        gates = base.put("gates", [P, NT, QH, 3], F32)
        ident_f = cst[:, C_ID:C_ID + P]
        diag_b, far_b = masks_b[:, 0:P], masks_b[:, P:2 * P]
        cmp_b = masks_b[:, 2 * P:].rearrange("p (t n) -> p t n", t=NT)
        START = base.at

        r1 = Region(nc, START)
        xth = r1.put("xth", [P, NK, S], F32R)
        xtl = r1.put("xtl", [P, NK, S], F32R)
        RW, RR = 13, 3
        wh = r1.put("wh", [P, RW, CH], F32R)
        wl = r1.put("wl", [P, RW, CH], F32R)
        wraw = r1.put("wraw", [P, RR, CH], F32)
        NST = 3
        stage = r1.put("stage", [P, NST, CH], F32)
        ropa = r1.put("ropa", [P, CH], F32)
        ropb = r1.put("ropb", [P, CH], F32)
        tab = r1.put("tab", [P, 4, NT, NA], F32)
        rstd = r1.put("rstd", [P, NT], F32)
        ms = r1.put("ms", [P, NT], F32)
        gnb = r1.put("gnb", [P, RH * HD], F32)
        ret_at = r1.at
        r = Region(nc, ret_at)
        rin = r.put("rin", [P, 4, CH], F32)
        q2_at = r.at
        q2 = r.put("q2", [P, RH, 2, HD], F32R)
        k2 = r.put("k2", [P, RH, 2, HD], F32R)
        kd = r.put("kd", [P, RH, HD], F32)
        kdh = r.put("kdh", [P, RH, 2, HD], F32R)
        kdl = r.put("kdl", [P, RH, 2, HD], F32R)
        vh_at = r.at
        vh = r.put("vh", [P, RH, HD], F32R)
        vl = r.put("vl", [P, RH, HD], F32R)
        qt = r.put("qt", [P, 4, P], F32R)
        ks = r.put("ks", [P, 4, P], F32R)
        kx = r.put("kx", [P, 4, P], F32R)
        sd = r.put("sd", [P, 4, P], F32)
        sth = r.put("sth", [P, 4, P], F32R)
        stl = r.put("stl", [P, 4, P], F32R)
        stf = r.put("stf", [P, RH, HD], F32)
        stt = r.put("stt", [P, RH, HD], F32)
        sh = r.put("sh", [P, RH, HD], F32R)
        sl = r.put("sl", [P, RH, HD], F32R)
        oc = r.put("oc", [P, RH, HD], F32)
        osq = r.put("osq", [P, RH, HD], F32)
        oout = r.put("oout", [P, RH, HD], F32)
        gst = r.put("gst", [P, 4, RH], F32)
        r = Region(nc, ret_at)
        XR = 4
        xraw = r.put("xraw", [P, XR, S], F32)
        xsq = r.put("xsq", [P, 2, S], F32)
        xacc = r.put("xacc", [P, S], F32)
        r = Region(nc, ret_at)
        posi = nc.alloc_sbuf_tensor_at("posi", [P, NT], I32, offset=r1.at + 44 * 1024)
        ang_r = Region(nc, r1.at + 44 * 1024 + 64)
        posf = ang_r.put("posf", [P, NT], F32)
        ang = ang_r.put("ang", [P, NT, NA], F32)
        turns = ang_r.put("turns", [P, NT, NA], F32)
        red = ang_r.put("red", [P, NT, NA], F32)
        red2 = ang_r.put("red2", [P, NT, NA], F32)
        ones = ang_r.put("ones", [P, 1], F32)

        a = Region(nc, START)
        nsah = a.put("nsah", [P, 4, S], F32R)
        nsal = a.put("nsal", [P, 4, S], F32R)
        reth = a.put("reth", [P, 4, S], F32R)
        retl = a.put("retl", [P, 4, S], F32R)
        OUT_AT = a.at
        aks = a.put("aks", [P, 2, G, S], F32R)
        akx = a.put("akx", [P, 2, G, S], F32R)
        av2 = a.put("av2", [P, 2, NT, G, 2 * HD], F32R)
        cks = a.put("cks", [P, G * NCMP + 2], F32R)
        ckx = a.put("ckx", [P, G * NCMP + 2], F32R)
        cv2 = a.put("cv2", [NCMP, G, 2 * HD], F32R)
        aro = a.put("aro", [P, 2, RH * HD], F32)
        PROB_AT = a.at
        NPR = S + (WIN_T + 1) * P + HD
        prob = a.put("prob", [P, 2, RG, NPR], F32)
        NPT = 2
        pth = a.put("pth", [P, NPT, 512], F32R)
        ptl = a.put("ptl", [P, NPT, 512], F32R)
        NPW = 2
        ptw = a.put("ptw", [P, NPW, 512], F32)
        aqr = a.put("aqr", [P, 2, RG * HD], F32)
        aq2 = a.put("aq2", [P, RG, 2, HD], F32R)
        aqt = a.put("aqt", [P, 2, 512], F32R)
        comb = a.put("comb", [P, 2, 2 * P], F32)
        mx = a.put("mx", [P, 4, 2], F32)
        nb = a.put("nb", [P, 4, 2], F32)
        den = a.put("den", [P, 4, 2], F32)
        rd = a.put("rd", [P, 4, 2], F32)
        rd2 = a.put("rd2", [P, 4, 2], F32)
        assert a.at <= 229344, a.at
        kraw = nc.alloc_sbuf_tensor_at("kraw", [P, NT, 4, P], F32, offset=q2_at)
        vraw = nc.alloc_sbuf_tensor_at("vraw", [P, NT, 2, P], F32, offset=ret_at)
        assert q2_at + NT * 4 * P * 4 <= vh_at and ret_at + NT * 2 * P * 4 <= q2_at
        b = Region(nc, q2_at + NT * 4 * P * 4)
        kspl = b.put("kspl", [P, 2, NT, G, 2, HD], F32R)
        b = Region(nc, START)
        cw1 = b.put("cw1", [P, 2, CJ, CMP_HID], F32)
        cb = b.put("cb", [P, 2, CJ, G * NCMP], F32)
        chidT = b.put("chidT", [P, 2, 2, G * NCMP], F32)
        cw2 = b.put("cw2", [P, 2, 2, HD], F32)
        cposb = b.put("cposb", [P, CJ], F32)
        c2 = b.put("c2", [G * NCMP, 2 * HD], F32R)

        o = Region(nc, OUT_AT)
        h = o.put("h", [P, NT, D], F32)
        LATE_AT = o.at
        OWR = 14
        owh = o.put("owh", [P, OWR, CH], F32R)
        owl = o.put("owl", [P, OWR, CH], F32R)
        owraw = o.put("owraw", [P, RR, CH], F32)
        hs = o.put("hs", [P, NT, D], F32)
        wfb = o.put("wfb", [P, D], F32)
        hst = o.put("hst", [P, 3, NT], F32)
        assert o.at <= 229344, o.at
        f = Region(nc, START)
        hth = f.put("hth", [P, NK, S], F32R)
        htl = f.put("htl", [P, NK, S], F32R)
        assert f.at == OUT_AT
        f = Region(nc, LATE_AT)
        wuraw = f.put("wuraw", [P, 2, NK // 2, 2 * P], F32)
        wuh = f.put("wuh", [P, 2, NK, 2 * P], F32R)
        wul = f.put("wul", [P, 2, NK, 2 * P], F32R)
        wdraw = f.put("wdraw", [P, D], F32)
        wdh = f.put("wdh", [P, 2, D], F32R)
        wdl = f.put("wdl", [P, 2, D], F32R)
        taps = f.put("taps", [P, 2, 4], F32)
        gate = f.put("gate", [P, S + 2], F32)
        act_ = f.put("act_", [P, S], F32)
        ffa = f.put("ffa", [P, S], F32)
        ffh = f.put("ffh", [P, 2, S], F32R)
        ffl = f.put("ffl", [P, 2, S], F32R)
        assert f.at <= 229344, f.at
        g = Region(nc, LATE_AT)
        GWR = 9
        gwh = g.put("gwh", [P, GWR, CH], F32R)
        gwl = g.put("gwl", [P, GWR, CH], F32R)
        pwh = g.put("pwh", [P, NP_, 2, CH], F32R)
        pwl = g.put("pwl", [P, NP_, 2, CH], F32R)
        peh = g.put("peh", [P, NP_, 2, CH], F32R)
        pel = g.put("pel", [P, NP_, 2, CH], F32R)
        sig = g.put("sig", [P, 2, CH], F32)
        pmul = g.put("pmul", [P, 2, CH], F32)
        ost = g.put("ost", [P, 2, D], F32)
        fwb = g.put("fwb", [P, D], F32)
        fst = g.put("fst", [P, 3, NT], F32)
        assert g.at >= f.at
        gwraw = g.put("gwraw", [P, RR, 2, CH], F32)
        assert g.at <= 229344, g.at

        cst_in = sem("cst_in")
        xt_in, w_in_s = sems("xt_in", XR), sems("w_in", RR)
        cst_r, cst_m = sem("cst_r"), sem("cst_m")
        xh_done, sq_done, xl_done = sem("xh_done"), sem("sq_done"), sem("xl_done")
        acc_done, ss_done, ms_done, rstd_done = sem("acc_done"), sem("ss_done"), sem("ms_done"), sem("rstd_done")
        red_done, sin_done = sem("red_done"), sem("sin_done")
        wh_done, wl_done, w_used = sem("wh_done"), sem("wl_done"), sem("w_used")
        pj_done, act_ev, dve_rd, dve_st = sem("pj_done"), sem("act_ev"), sem("dve_rd"), sem("dve_st")
        copy_ev = sem("copy_ev")
        store_s = sems("store", NST)
        dve_chain = sem("dve_chain")
        rin_s = sems("rin", 4)
        q2h_done, q2l_done, k2h_done, k2l_done = sem("q2h_done"), sem("q2l_done"), sem("k2h_done"), sem("k2l_done")
        vh_done, vl_done = sem("vh_done"), sem("vl_done")
        kd_done, kdh_done, kdl_done = sem("kd_done"), sem("kdh_done"), sem("kdl_done")
        tq_done, tk_done, qt_done, ks_done, kx_done = sem("tq_done"), sem("tk_done"), sem("qt_done"), sem("ks_done"), sem("kx_done")
        sc_done, sd_done, sth_done, stl_done = sem("sc_done"), sem("sd_done"), sem("sth_done"), sem("stl_done")
        cr_done, kv_done, in_done = sem("cr_done"), sem("kv_done"), sem("in_done")
        st_done, sh_done, sl_done = sem("st_done"), sem("sh_done"), sem("sl_done")
        oread, osub_done, osq_done, var_done, orstd_done, oout_done = (
            sem("oread"), sem("osub_done"), sem("osq_done"), sem("var_done"), sem("orstd_done"), sem("oout_done"))
        reto_s = sem("reto_s")

        NS = NCH * NT
        DVE_CH, ACT_CH = (0, 1, 4, 5), (2, 3, 6)

        def dve_steps(s):
            return sum(u // NT in DVE_CH for u in range(s))

        def act_steps(s):
            return sum(u // NT in ACT_CH for u in range(s))

        def copy_steps(s):
            return sum(u // NT in (4, 5) for u in range(s))

        def stored(eng, s):
            eng.wait_ge(store_s[s % NST], 16 * (s // NST + 1))

        def slice_at(s, k):
            c, t = divmod(s, NT)
            if c + 1 < NCH:
                late = RW - NK
                if t < late and k == 3:
                    return NT * (c + 1) + t
                if t == NT - 1 and 2 <= k < 2 + NT - late:
                    return NT * (c + 1) + late + k - 2
            return None

        RET0 = 21 * NK
        RSLOTS = 32

        def ret_slots(s, k, table):
            m = s * NK + k - RET0
            for r in (m // RSLOTS - 1, m // RSLOTS):
                if 0 <= r < NT:
                    for fn, args in table.get(m - RSLOTS * r, ()):
                        fn(r, *args)

        kraw_in, vraw_in, cpos_in, comp_in = sem("kraw_in"), sem("vraw_in"), sem("cpos_in"), sems("comp_in", 2)
        kt_done, cb_done, hid_done, gelu_done = sem("kt_done"), sem("cb_done"), sem("hid_done"), sem("gelu_done")
        ck_done, ckh_done, ckl_done, ckt_done, cks_done, ckx_done = (
            sem("ck_done"), sem("ckh_done"), sem("ckl_done"), sem("ckt_done"), sem("cks_done"), sem("ckx_done"))
        kh_done, kl_done, kk_done, aks_done, akx_done, akx2_done = (
            sem("kh_done"), sem("kl_done"), sem("kk_done"), sem("aks_done"), sem("akx_done"), sem("akx2_done"))
        aqr_in, aro_in = sems("aqr_in", 2), sems("aro_in", 2)
        aqh_done, aql_done = sem("aqh_done"), sem("aql_done")
        tr_full, tr_h, tr_l = sem("tr_full"), sem("tr_h"), sem("tr_l")
        qk_done, nb_done, exp_done, norm_done, pv_done = (
            sem("qk_done"), sem("nb_done"), sem("exp_done"), sem("norm_done"), sem("pv_done"))
        swap_done, csum_done, nsah_done, nsal_done = sem("swap_done"), sem("csum_done"), sem("nsah_done"), sem("nsal_done")
        h_in, wfb_in = sem("h_in"), sem("wfb_in")
        owh_done, owl_done, ow_used, op_done, op_add = sem("owh_done"), sem("owl_done"), sem("ow_used"), sem("op_done"), sem("op_add")
        hsq_done, hms_done, hrs_done, hs_done = sem("hsq_done"), sem("hms_done"), sem("hrs_done"), sem("hs_done")
        ht_full, ht_h, ht_l = sem("ht_full"), sem("ht_h"), sem("ht_l")
        wu_in, wd_in, taps_in = sems("wu_in", 2), sem("wd_in"), sems("taps_in", 2)
        wuh_done, wul_done, wdh_done, wdl_done = sem("wuh_done"), sem("wul_done"), sem("wdh_done"), sem("wdl_done")
        up_g, up_v, gate_ev, tap_done, conv_done, silu_done = (
            sem("up_g"), sem("up_v"), sem("gate_ev"), sem("tap_done"), sem("conv_done"), sem("silu_done"))
        ffa_done, ffh_done, ffl_done, dn_done, dn_add = sem("ffa_done"), sem("ffh_done"), sem("ffl_done"), sem("dn_done"), sem("dn_add")
        conv_mid = sem("conv_mid")
        gwh_done, gwl_done, gw_used = sem("gwh_done"), sem("gwl_done"), sem("gw_used")
        gt_full, gt_h, gt_l = sem("gt_full"), sem("gt_h"), sem("gt_l")
        pg_done, sig_done, pmul_done, pg_add = sem("pg_done"), sem("sig_done"), sem("pmul_done"), sem("pg_add")
        fsq_done, fms_done, frs_done, fin_done = sem("fsq_done"), sem("fms_done"), sem("frs_done"), sem("fin_done")
        out_s = sems("out_s", 2)

        NV = NT * G

        def key_tiles(v):
            t = v // G
            w0 = max(0, t - WIN_T)
            return ([(0, j, j * P, P) for j in range(t + 1)]
                    + [(1, j, S + (j - w0) * P, P) for j in range(w0, t + 1)]
                    + [(2, 0, S + (WIN_T + 1) * P, NCMP)])

        def plan_attention():
            per = 2 * RG
            slots = [[] for _ in range(per * (NV + 1) + 3)]
            for v in range(NV):
                base = per * (v + 1) + 1
                tail = []
                if v % 2 == 0:
                    tail.append(("turn_ret", v // 2))
                n = len(key_tiles(v))
                for j in range(n + 2):
                    if j < n:
                        tail.append(("turn_p", v, j))
                    if j >= 2:
                        tail.append(("output", v, j - 2))
                for x, st in enumerate(tail):
                    slots[base + per * x // len(tail)].append(st)
                slots[base + per - 1].append(("sum", v))
                slots[base + per].append(("combine", v))
                if v + 1 < NV:
                    slots[per * v].append(("split_q", v + 1))
                    slots[per * v + RG].append(("turn_q", v + 1))
            return slots

        slots = plan_attention()
        plan = [("split_q", 0), ("turn_q", 0)] + [st for slot in slots for st in slot]
        turns_of = {st: n for n, st in enumerate(st for st in plan if st[0].startswith("turn"))}
        def whole(st):
            return st[0] == "turn_p" and st[2] % 5 in (0, 2)

        outs_of = {(v, j): n for n, (v, j) in enumerate(st[1:] for st in plan if st[0] == "output")}
        place_of, freed_by = {}, {}
        for kind, ring in ((False, NPT), (True, NPW)):
            same = [st for st in plan if st[0] == "turn_p" and whole(st) == kind]
            for n, st in enumerate(same):
                place_of[st] = n % ring
                freed_by[st] = outs_of[same[n - ring][1:]] + 1 if n >= ring else 0
        turn_list = sorted(turns_of, key=turns_of.get)

        NTR = 3

        def skip(st):
            pass

        def low_of(n):
            return sum(not (st[0] == "turn_q" or whole(st)) for st in turn_list[:n])

        def turn_bank(st):
            return 4 + turns_of[st] % NTR

        def late_slice(n, k, ring):
            if n == NT - 1 and 1 <= k and k - 1 + ring < 2 * NK:
                return k - 1 + ring
            return None

        OPS = 2 * NT

        def raw_slice(eng, j, *before):
            eng.wait_ge(w_in_s[j % RR], 16 * (j // RR + 1 + sum((n - j % RR + RR - 1) // RR for n in before)))

        def part_of(j, pe_, pw_, gw_):
            if j < 2 * NP_:
                return pe_[:, j // 2, j % 2]
            if j < 4 * NP_:
                return pw_[:, (j - 2 * NP_) // 2, j % 2]
            return gw_[:, (j - 4 * NP_) % GWR]

        def bc(ap, shape):
            return ap.to_broadcast(shape)

        block = ctx.enter_context(nc.Block())

        @block.sync
        def _(sp):
            sp.dma_start(cst[:], cst_d).then_inc(cst_in, 16)
            sp.dma_start(wmix[:], wmix_d).then_inc(cst_in, 16)
            sp.dma_start(posi[:], pos).then_inc(cst_in, 16)

            def load_slice(j):
                if j >= RR:
                    sp.wait_ge(wl_done, j - RR + 1)
                c, k = divmod(j, NK)
                sp.dma_start(wraw[:, j % RR, 0:CW[c]], w_in[:, (c * NK + k) * CH:(c * NK + k) * CH + CW[c]]) \
                    .then_inc(w_in_s[j % RR], 16)

            def load_x(k):
                if k >= NK:
                    return
                if k >= XR:
                    sp.wait_ge(xl_done, k - XR + 1)
                    sp.wait_ge(sq_done, k - XR + 1)
                sp.dma_start(xraw[:, k % XR], xt[k * P:(k + 1) * P, :]).then_inc(xt_in[k % XR], 16)

            load_x(0)
            load_x(1)
            for k in range(NK):
                load_slice(k)
                load_x(k + 2)
            sp.dma_start(gnb[:], gnw.partition_broadcast(P)).then_inc(cst_in, 16)
            for j in range(NK, NCH * NK):
                load_slice(j)

            sp.wait_ge(tk_done, 2 * NT)
            sp.wait_ge(tq_done, 2 * NT)
            sp.wait_ge(kd_done, NT)
            sp.wait_ge(kv_done, NT - 1)
            for s in range(6 * NT - NST, 6 * NT):
                stored(sp, s)
            part = lambda c, n: proj_d[:, c * CH:c * CH + n * P].rearrange("(t p) (a c) -> p t a c", p=P, a=n)
            sp.dma_start(kraw[:], part(5, 4)).then_inc(kraw_in, 16)
            sp.wait_ge(pj_done, NS)
            sp.dma_start(cposb[:], cpos).then_inc(cpos_in, 16)
            for i in range(2):
                sp.dma_start(cw1[:, i], (ck_w1, cv_w1)[i].rearrange("(j p) n -> p j n", p=P)).then_inc(comp_in[i], 16)
                sp.dma_start(cw2[:, i], (ck_w2, cv_w2)[i].rearrange("(j p) n -> p j n", p=P)).then_inc(comp_in[i], 16)
            for s in range(NS - NST, NS):
                stored(sp, s)
            sp.wait_ge(reto_s, 16 * NT)
            sp.dma_start(vraw[:], part(6, 2)).then_inc(vraw_in, 16)

            def load_q(v):
                if v >= 2:
                    sp.wait_ge(aql_done, v - 1)
                t, g_ = divmod(v, G)
                at = 4 * CH + g_ * RG * HD
                sp.dma_start(aqr[:, v % 2], proj_d[t * P:(t + 1) * P, at:at + RG * HD]).then_inc(aqr_in[v % 2], 16)

            def load_ret(t):
                if t >= 2:
                    sp.wait_ge(tr_full, turns_of["turn_ret", t - 2] + 1)
                sp.dma_start(aro[:, t % 2], reto_d[t * P:(t + 1) * P, :]).then_inc(aro_in[t % 2], 16)

            for v in range(NV):
                load_q(v)
                if v % 2 == 0:
                    load_ret(v // 2)

            sp.wait_ge(qk_done, 2 * RG * NV)
            sp.dma_start(h[:], x.rearrange("(t p) d -> p t d", p=P)).then_inc(h_in, 16)
            sp.wait_ge(pv_done, len(outs_of))
            for j in range(2 * NK):
                if j >= RR:
                    sp.wait_ge(owl_done, j - RR + 1)
                half, k = divmod(j, NK)
                sp.dma_start(owraw[:, j % RR], w_out[k * P:(k + 1) * P, half * CH:(half + 1) * CH]).then_inc(w_in_s[j % RR], 16)
                if j == NK:
                    sp.dma_start(wfb[:], wffn_d.partition_broadcast(P)).then_inc(wfb_in, 16)

            def ffn_load(f, u, q, first):
                for i in range(2):
                    if not first:
                        sp.wait_ge(wul_done, 2 * f + i - 1)
                    sp.dma_start(wuraw[:, i], w_up[bass.ds(f, 1), :, i * NK * P:(i + 1) * NK * P]
                                 .rearrange("o p (k n) -> p (o k) n", n=2 * P)).then_inc(wu_in[i], 16)
                if not first:
                    sp.wait_ge(wdl_done, f)
                sp.dma_start(wdraw[:], w_down[bass.ds(f, 1)].rearrange("o p n -> p (o n)")).then_inc(wd_in, 16)
                if q is not None:
                    sp.wait_ge(conv_done, f - 1)
                sp.dma_start(taps[:, u], conv_d[bass.ds(f, 1)].rearrange("o p n -> p (o n)")).then_inc(taps_in[u], 16)

            sp.wait_ge(op_done, OPS)
            ffn_load(0, 0, None, True)
            ffn_load(1, 1, None, False)
            with sp.Fori(0, NF // 2 - 1) as i:
                ffn_load(2 * i + 2, 0, i + 1, False)
                ffn_load(2 * i + 3, 1, i + 1, False)

            for m in range(2 * NP_ + NK):
                if m >= RR:
                    sp.wait_ge(gwl_done, 2 * (m - RR + 1))
                if m < 2 * NP_:
                    src, k = (pt if m < NP_ else ple_w), m % NP_
                    pair = src[k * P:(k + 1) * P, :].rearrange("p (a n) -> p a n", a=2)
                else:
                    half, k = divmod(2 * (m - 2 * NP_), NK)
                    pair = ple_gw[k * P:(k + 2) * P, half * CH:(half + 1) * CH].rearrange("(a p) n -> p a n", p=P)
                sp.dma_start(gwraw[:, m % RR], pair).then_inc(w_in_s[m % RR], 16)
            sp.dma_start(fwb[:], fnw.partition_broadcast(P)).then_inc(wfb_in, 16)
            for t in range(NT):
                sp.wait_ge(fin_done, t + 1)
                sp.dma_start(out[t * P:(t + 1) * P, :], ost[:, t % 2]).then_inc(out_s[t % 2], 16)
            for i in range(2):
                sp.wait_ge(out_s[i], 16 * (NT // 2))

        @block.gpsimd
        def _(pool):
            for k in range(1, NK):
                pool.wait_ge(sq_done, k + 1)
                if k > 1:
                    pool.wait_ge(acc_done, k - 1)
                nc.gpsimd.tensor_tensor(xacc[:], xacc[:] if k > 1 else xsq[:, 0], xsq[:, k % 2], ALU.add).then_inc(acc_done, 1)
            pool.wait_ge(ms_done, 1)
            nc.gpsimd.tensor_tensor(rstd[:], ms[:], cst[:, C_HALF:C_HALF + NT], ALU.pow).then_inc(rstd_done, 1)

            def store(s):
                c, t = divmod(s, NT)
                n = CH if c < 6 else 2 * P
                if c in DVE_CH:
                    pool.wait_ge(dve_st, dve_steps(s + 1))
                else:
                    pool.wait_ge(act_ev, act_steps(s + 1))
                pool.dma_start(proj_d[t * P:(t + 1) * P, c * CH:c * CH + n], stage[:, s % NST, 0:n]) \
                    .then_inc(store_s[s % NST], 16)

            def ret_load(r):
                if r == NT:
                    return
                for i, free in enumerate((q2l_done, kd_done, vl_done)):
                    stored(pool, i * NT + r)
                    if i == 1 and r:
                        pool.wait_ge(k2l_done, r)
                    if r:
                        pool.wait_ge(free, r)
                    pool.dma_start(rin[:, i], proj_d[r * P:(r + 1) * P, i * CH:(i + 1) * CH]).then_inc(rin_s[i], 16)

            def ret_gate(r):
                stored(pool, 3 * NT + r)
                if r:
                    pool.wait_ge(oout_done, r)
                pool.dma_start(rin[:, 3], proj_d[r * P:(r + 1) * P, 3 * CH:4 * CH]).then_inc(rin_s[3], 16)

            def ret_norm(r):
                pool.wait_ge(var_done, r + 1)
                nc.gpsimd.tensor_tensor(gst[:, 3], gst[:, 2], cst[:, C_HALF:C_HALF + RH], ALU.pow).then_inc(orstd_done, 1)

            def ret_store(r):
                pool.wait_ge(oout_done, r + 1)
                pool.dma_start(reto_d[r * P:(r + 1) * P, :], oout[:].rearrange("p a d -> p (a d)")).then_inc(reto_s, 16)

            def ret_load_next(r):
                ret_load(r + 1)

            table = {16: [(ret_load_next, ())], 36: [(ret_gate, ())], 43: [(ret_norm, ())], 48: [(ret_store, ())]}
            for s in range(NS + 1):
                for k in range(NK):
                    if k == 0 and s >= 1:
                        store(s - 1)
                    if s * NK + k == RET0 - 4:
                        ret_load(0)
                    ret_slots(s, k, table)

            for t in range(NT):
                pool.wait_ge(hms_done, t + 1)
                nc.gpsimd.tensor_tensor(hst[:, 2, t:t + 1], hst[:, 1, t:t + 1], cst[:, C_HALF:C_HALF + 1], ALU.pow) \
                    .then_inc(hrs_done, 1)
            for t in range(NT):
                pool.wait_ge(fms_done, t + 1)
                nc.gpsimd.tensor_tensor(fst[:, 2, t:t + 1], fst[:, 1, t:t + 1], cst[:, C_HALF:C_HALF + 1], ALU.pow) \
                    .then_inc(frs_done, 1)

        @block.scalar
        def _(act):
            act.wait_ge(cst_in, 48)
            nc.scalar.activation(ident_r[:], ident_f, ACT.Copy).then_inc(cst_r, 1)

            def split_w(j):
                raw_slice(act, j)
                if j >= RW:
                    act.wait_ge(w_used, j - RW + 1)
                n = CW[j // NK]
                nc.scalar.activation(wh[:, j % RW, 0:n], wraw[:, j % RR, 0:n], ACT.Copy).then_inc(wh_done, 1)

            for k in range(NK):
                act.wait_ge(xt_in[k % XR], 16 * (k // XR + 1))
                nc.scalar.activation(xth[:, k], xraw[:, k % XR], ACT.Copy, scale=wmix[:, k:k + 1]).then_inc(xh_done, 1)
                if k >= 2:
                    act.wait_ge(acc_done, max(1, k - 2))
                nc.scalar.activation(xsq[:, k % 2], xraw[:, k % XR], ACT.Square).then_inc(sq_done, 1)
                split_w(k)
            act.wait_ge(red_done, 1)
            nc.scalar.activation(tab[:, 1], red[:], ACT.Sin).then_inc(sin_done, 1)
            act.wait_ge(red_done, 2)
            nc.scalar.activation(tab[:, 0], red2[:], ACT.Sin).then_inc(sin_done, 1)

            def evac(s):
                c, t = divmod(s, NT)
                if c not in ACT_CH and c not in (4, 5):
                    return
                act.wait_ge(pj_done, s + 1)
                act.wait_ge(rstd_done, 1)
                if s >= NST:
                    stored(act, s - NST)
                src, dst, by = ps[:, s % 2, :], stage[:, s % NST, :], rstd[:, t:t + 1]
                if c in (4, 5):
                    nc.scalar.activation(dst, src, ACT.Copy, scale=by).then_inc(copy_ev, 1)
                elif c == 2:
                    nc.scalar.activation(dst, src, ACT.Copy, scale=by).then_inc(act_ev, 1)
                elif c == 3:
                    nc.scalar.activation(dst, src, ACT.Silu, scale=by).then_inc(act_ev, 1)
                else:
                    nc.scalar.activation(dst[:, 0:2 * P], src[:, 0:2 * P], ACT.Copy, scale=by)
                    nc.scalar.activation(gates[:, t].rearrange("p a b -> p (a b)"), src[:, 2 * P:2 * P + 3 * QH],
                                         ACT.Sigmoid, scale=by).then_inc(act_ev, 1)

            def heads(i):
                return rin[:, i].rearrange("p (a d) -> p a d", a=RH)

            def q_high(r):
                act.wait_ge(rin_s[0], 16 * (r + 1))
                if r:
                    act.wait_ge(tq_done, 2 * r)
                nc.scalar.activation(q2[:, :, 0], heads(0), ACT.Copy).then_inc(q2h_done, 1)

            def k_high(r):
                act.wait_ge(rin_s[1], 16 * (r + 1))
                if r:
                    act.wait_ge(tk_done, 2 * r)
                nc.scalar.activation(k2[:, :, 0], heads(1), ACT.Copy).then_inc(k2h_done, 1)

            def v_high(r):
                act.wait_ge(rin_s[2], 16 * (r + 1))
                if r:
                    act.wait_ge(in_done, 2 * r)
                    act.wait_ge(kv_done, r)
                nc.scalar.activation(vh[:], heads(2), ACT.Copy).then_inc(vh_done, 1)

            def kd_high(r):
                if r == NT - 1:
                    return
                act.wait_ge(kd_done, r + 1)
                if r:
                    act.wait_ge(kv_done, r)
                nc.scalar.activation(kdh[:], bc(kd[:].rearrange("p a (o d) -> p a o d", o=1), [P, RH, 2, HD]),
                                     ACT.Copy).then_inc(kdh_done, 1)

            def qt_copy(r, f):
                n = 2 * r + f
                act.wait_ge(tq_done, n + 1)
                if n:
                    act.wait_ge(sc_done, n)
                    if n > 2:
                        act.wait_ge(cr_done, n - 2)
                nc.scalar.activation(qt[:].rearrange("p a d -> p (a d)"), ps[:, 2, :], ACT.Copy).then_inc(qt_done, 1)

            def kx_copy(r, f):
                n = 2 * r + f
                act.wait_ge(ks_done, n + 1)
                if n:
                    act.wait_ge(sc_done, n)
                nc.scalar.activation(kx[HD:P], ks[0:HD].bitcast(F32), ACT.Copy)
                nc.scalar.activation(kx[0:HD], ks[HD:P].bitcast(F32), ACT.Copy).then_inc(kx_done, 1)

            def st_high(r, f):
                n = 2 * r + f
                act.wait_ge(sd_done, n + 1)
                if n:
                    act.wait_ge(in_done, n)
                nc.scalar.activation(sth[:], sd[:], ACT.Copy).then_inc(sth_done, 1)

            def state_high(r):
                if r == NT - 1:
                    return
                act.wait_ge(st_done, r + 1)
                if r:
                    act.wait_ge(cr_done, 2 * r)
                nc.scalar.activation(sh[:], stf[:], ACT.Copy).then_inc(sh_done, 1)

            def o_square(r):
                act.wait_ge(osub_done, r + 1)
                nc.scalar.activation(osq[:], oc[:], ACT.Square).then_inc(osq_done, 1)

            table = {0: [(q_high, ())], 1: [(k_high, ())], 2: [(v_high, ())], 3: [(kd_high, ())],
                     5: [(qt_copy, (0,))], 7: [(kx_copy, (0,))], 12: [(st_high, (0,))],
                     18: [(qt_copy, (1,))], 20: [(kx_copy, (1,))], 24: [(st_high, (1,))], 26: [(state_high, ())],
                     41: [(o_square, ())]}
            for s in range(NS + 1):
                for k in range(NK):
                    if k == 0 and s >= 1:
                        evac(s - 1)
                    if s < NS and (j := slice_at(s, k)) is not None:
                        split_w(j)
                    ret_slots(s, k, table)

            act.wait_ge(in_done, 2 * NT)
            act.wait_ge(kraw_in, 16)
            gd = lambda ap: ap.rearrange("p t (g d) -> p t g d", g=G)
            for i in range(2):
                nc.scalar.activation(kspl[:, i, :, :, 0], gd(kraw[:, :, 1 + i]), ACT.Copy).then_inc(kh_done, 1)
            for e in range(8):
                br, g_, q4 = e // 4, e // 2 % 2, e % 2
                act.wait_ge(kk_done, e + 1)
                nc.scalar.activation(aks[:, br, g_, q4 * 512:(q4 + 1) * 512], ps[:, 4 + e % 2, :], ACT.Copy).then_inc(aks_done, 1)
                act.wait_ge(aks_done, e + 1)
                nc.scalar.activation(akx[HD:P, br, g_, q4 * 512:(q4 + 1) * 512],
                                     aks[0:HD, br, g_, q4 * 512:(q4 + 1) * 512].bitcast(F32), ACT.Copy).then_inc(akx_done, 1)
            act.wait_ge(vraw_in, 16)
            for i in range(2):
                nc.scalar.activation(av2[:, i, :, :, 0:HD], gd(vraw[:, :, i]), ACT.Copy).then_inc(kh_done, 1)
            for i in range(2):
                act.wait_ge(hid_done, i + 1)
                nc.scalar.activation(chidT[:, i].rearrange("p b n -> p (b n)"), ps[:, 6 + i, 0:2 * G * NCMP], ACT.Gelu_apprx_tanh) \
                    .then_inc(gelu_done, 1)
            act.wait_ge(ck_done, 1)
            nc.scalar.activation(c2[:, 0:HD], ps[0:G * NCMP, 1, 0:HD], ACT.Copy)
            nc.scalar.activation(cv2[:, :, 0:HD], ps[0:NCMP, 1, P:2 * P].rearrange("p (g d) -> p g d", g=G), ACT.Copy) \
                .then_inc(ckh_done, 1)
            act.wait_ge(cks_done, 1)
            nc.scalar.activation(ckx[HD:P], cks[0:HD].bitcast(F32), ACT.Copy)
            nc.scalar.activation(ckx[0:HD], cks[HD:P].bitcast(F32), ACT.Copy).then_inc(ckx_done, 1)

            def q_split_high(st):
                v = st[1]
                act.wait_ge(aqr_in[v % 2], 16 * (v // 2 + 1))
                if v:
                    act.wait_ge(tr_full, turns_of["turn_q", v - 1] + 1)
                nc.scalar.activation(aq2[:, :, 0], aqr[:, v % 2].rearrange("p (r d) -> p r d", r=RG), ACT.Copy).then_inc(aqh_done, 1)

            def q_turned(st):
                v = st[1]
                act.wait_ge(tr_full, turns_of[st] + 1)
                if v >= 2:
                    act.wait_ge(qk_done, 2 * RG * (v - 1))
                nc.scalar.activation(aqt[:, v % 2], ps[:, turn_bank(st), :], ACT.Copy).then_inc(tr_h, 1)

            def exponentials(v, i):
                n, t = 2 * RG * v + i, v // G
                r_, br = divmod(i, 2)
                act.wait_ge(nb_done, n + 1)
                if v >= 2:
                    act.wait_ge(tr_full, turns_of["turn_p", v - 2, len(key_tiles(v - 2)) - 1] + 1)
                s_, pr = ps[:, 2 * br:2 * br + 2, :].rearrange("p a n -> p (a n)"), prob[:, v % 2, r_]
                m = n % 4
                if br == 0:
                    nc.scalar.activation(pr[:, 0:(t + 1) * P], s_[:, 0:(t + 1) * P], ACT.Exp, bias=nb[:, m, 0:1],
                                         scale=SCALE, accum_out=den[:, m, 0:1]).then_inc(exp_done, 1)
                else:
                    w = (t - max(0, t - WIN_T) + 1) * P
                    nc.scalar.activation(pr[:, S:S + w], s_[:, 0:w], ACT.Exp, bias=nb[:, m, 0:1], scale=SCALE,
                                         accum_out=den[:, m, 0:1])
                    at = S + (WIN_T + 1) * P
                    nc.scalar.activation(pr[:, at:at + NCMP], s_[:, 5 * P:5 * P + NCMP], ACT.Exp, bias=nb[:, m, 1:2],
                                         scale=SCALE, accum_out=den[:, m, 1:2]).then_inc(exp_done, 1)

            def p_high(st):
                at = place_of[st]
                w = key_tiles(st[1])[st[2]][3]
                act.wait_ge(tr_full, turns_of[st] + 1)
                if freed_by[st]:
                    act.wait_ge(pv_done, freed_by[st])
                to = ptw[0:w, at] if whole(st) else pth[0:w, at]
                nc.scalar.activation(to, ps[0:w, turn_bank(st), :], ACT.Copy).then_inc(tr_h, 1)

            def ret_high(st):
                t = st[1]
                act.wait_ge(tr_full, turns_of[st] + 1)
                nc.scalar.activation(reth[:, :, t * P:(t + 1) * P], ps[:, turn_bank(st), :].rearrange("p (k n) -> p k n", k=4),
                                     ACT.Copy).then_inc(tr_h, 1)

            def swap(st):
                v = st[1]
                act.wait_ge(pv_done, outs_of[v, len(key_tiles(v)) - 1] + 1)
                if v:
                    act.wait_ge(csum_done, v)
                o_ = ps[:, 7, :].rearrange("p (a b n) -> p a b n", a=2, b=2)
                c_ = comb[:, 0].rearrange("p (a n) -> p a n", a=2)
                nc.scalar.activation(c_[0:HD], o_[HD:P, :, 0], ACT.Copy)
                nc.scalar.activation(c_[HD:P], o_[0:HD, :, 1], ACT.Copy).then_inc(swap_done, 1)

            def nsa_high(st):
                v = st[1]
                t, g_ = divmod(v, G)
                act.wait_ge(csum_done, v + 1)
                nc.scalar.activation(nsah[:, 2 * g_:2 * g_ + 2, t * P:(t + 1) * P],
                                     comb[:, 1].rearrange("p (a n) -> p a n", a=2), ACT.Copy).then_inc(nsah_done, 1)

            q_split_high(("split_q", 0))
            q_turned(("turn_q", 0))
            for n, slot in enumerate(slots):
                for st in slot:
                    {"split_q": q_split_high, "turn_q": q_turned, "turn_p": p_high, "turn_ret": ret_high,
                     "sum": swap, "combine": nsa_high}.get(st[0], skip)(st)
                if n < 2 * RG * NV:
                    exponentials(*divmod(n, 2 * RG))

            def ow_high(j):
                raw_slice(act, j, NCH * NK)
                if j >= OWR:
                    act.wait_ge(ow_used, j - OWR + 1)
                nc.scalar.activation(owh[:, j % OWR], owraw[:, j % RR], ACT.Copy).then_inc(owh_done, 1)

            for j in range(OWR):
                ow_high(j)
            for n in range(OPS):
                for k in range(NK):
                    if (j := late_slice(n, k, OWR)) is not None:
                        ow_high(j)
                if n >= NT:
                    t = n - NT
                    act.wait_ge(op_add, n + 1)
                    nc.scalar.activation(hs[:, t], h[:, t], ACT.Square, accum_out=hst[:, 0, t:t + 1]).then_inc(hsq_done, 1)
            for e in range(2 * NT):
                t, q = divmod(e, 2)
                act.wait_ge(ht_full, e + 1)
                nc.scalar.activation(hth[:, 4 * q:4 * q + 4, t * P:(t + 1) * P],
                                     ps[:, 4 + e % 4, :].rearrange("p (k n) -> p k n", k=4), ACT.Copy).then_inc(ht_h, 1)

            def wu_high(f, u, first):
                for i in range(2):
                    act.wait_ge(wu_in[i], 16 * f + 16)
                    if i == 0 and not first:
                        act.wait_ge(up_v, f - 1)
                    nc.scalar.activation(wuh[:, u, i * 4:i * 4 + 4], wuraw[:, i], ACT.Copy).then_inc(wuh_done, 1)

            def wd_high(f, u, first):
                act.wait_ge(wd_in, 16 * f + 16)
                if not first:
                    act.wait_ge(dn_done, OPS * f - OPS)
                nc.scalar.activation(wdh[:, u], wdraw[:], ACT.Copy).then_inc(wdh_done, 1)

            def ffn_act(f, u, q, first, last=False):
                if not last:
                    wu_high(f + 1, 1 - u, first == 0)
                act.wait_ge(up_g, f + 1)
                if first != 0:
                    act.wait_ge(conv_done, f)
                nc.scalar.activation(gate[:, 2:S + 2], ps[:, 0:2, :].rearrange("p a n -> p (a n)"), ACT.Copy).then_inc(gate_ev, 1)
                act.wait_ge(gate_ev, f + 1)
                act.wait_ge(taps_in[u], 16 * q + 16)
                if first != 0:
                    act.wait_ge(ffa_done, f)
                nc.scalar.activation(act_[:], gate[:, 2:S + 2], ACT.Identity, scale=taps[:, u, 2:3],
                                     bias=taps[:, u, 3:4]).then_inc(tap_done, 1)
                act.wait_ge(conv_done, f + 1)
                nc.scalar.activation(act_[:], act_[:], ACT.Silu).then_inc(silu_done, 1)
                act.wait_ge(ffa_done, f + 1)
                if first is None:
                    act.wait_ge(dn_done, OPS * f - OPS)
                nc.scalar.activation(ffh[:, u], ffa[:], ACT.Copy).then_inc(ffh_done, 1)
                if not last:
                    wd_high(f + 1, 1 - u, first == 0)

            wu_high(0, 0, True)
            wd_high(0, 0, True)
            ffn_act(0, 0, 0, 0)
            ffn_act(1, 1, 0, 1)
            with act.Fori(0, NF // 2 - 2) as i:
                ffn_act(2 * i + 2, 0, i + 1, None)
                ffn_act(2 * i + 3, 1, i + 1, None)
            ffn_act(NF - 2, 0, NF // 2 - 1, None)
            ffn_act(NF - 1, 1, NF // 2 - 1, None, last=True)

            def gw_high(j):
                raw_slice(act, j // 2, NCH * NK, 2 * NK)
                n = j - 4 * NP_
                if n >= GWR:
                    act.wait_ge(gw_used, n - GWR + 1)
                nc.scalar.activation(part_of(j, peh, pwh, gwh), gwraw[:, j // 2 % RR, j % 2], ACT.Copy).then_inc(gwh_done, 1)

            def gt_high(e):
                t, q = divmod(e, 2)
                act.wait_ge(gt_full, e + 1)
                nc.scalar.activation(hth[:, 4 * q:4 * q + 4, t * P:(t + 1) * P],
                                     ps[:, 4 + e % 4, :].rearrange("p (k n) -> p k n", k=4), ACT.Copy).then_inc(gt_h, 1)

            def square_out(t):
                act.wait_ge(pg_add, NT + t + 1)
                if t >= 2:
                    act.wait_ge(out_s[t % 2], 16 * (t // 2))
                nc.scalar.activation(ost[:, t % 2], h[:, t], ACT.Square, accum_out=fst[:, 0, t:t + 1]).then_inc(fsq_done, 1)

            act.wait_ge(dn_done, OPS * NF)
            for j in range(4 * NP_ + GWR):
                gw_high(j)
                if j in (1, 3):
                    gt_high(j // 2)
            for n in range(OPS):
                if 0 < n < NT:
                    gt_high(2 * n)
                    gt_high(2 * n + 1)
                for k in range(NK):
                    if (j := late_slice(n, k, GWR)) is not None:
                        gw_high(4 * NP_ + j)
                act.wait_ge(pg_done, n + 1)
                if n >= 2:
                    act.wait_ge(pmul_done, n - 1)
                nc.scalar.activation(sig[:, n % 2], ps[:, n % 2, :], ACT.Sigmoid).then_inc(sig_done, 1)
                if n > NT:
                    square_out(n - NT - 1)
            square_out(NT - 1)

        @block.tensor
        def _(pe):
            def product(out, wts, xs, start, stop):
                (wh_, wl_), (xh_, xl_) = wts, xs
                first = nc.tensor.matmul(out, wh_, xh_, start=start, stop=False)
                nc.tensor.matmul(out, wh_, xl_, start=False, stop=False)
                return first, nc.tensor.matmul(out, wl_, xh_, start=False, stop=stop)

            def transpose_r(out, in_):
                return nc.tensor.transpose(out.bitcast(F32R), in_, ident_r[:])

            def project(s, k):
                c, t = divmod(s, NT)
                n = CW[c]
                j = c * NK + k
                if s == 0:
                    pe.wait_ge(xl_done, k + 1)
                if t == 0:
                    pe.wait_ge(wl_done, j + 1)
                if k == 0 and s >= 2:
                    u = s - 2
                    if u // NT in DVE_CH:
                        pe.wait_ge(dve_rd, dve_steps(u + 1))
                    else:
                        pe.wait_ge(act_ev, act_steps(u + 1))
                tok = slice(t * P, (t + 1) * P)
                first, last = product(ps[:, s % 2, 0:n], (xth[:, k, tok], xtl[:, k, tok]),
                                      (wh[:, j % RW, 0:n], wl[:, j % RW, 0:n]), k == 0, k == NK - 1)
                if (t == NT - 1 and k > 0) or (t == 0 and k == 0 and s > 0):
                    first.then_inc(w_used, 1)
                if k == NK - 1:
                    last.then_inc(pj_done, 1)

            def sum_squares():
                pe.wait_ge(acc_done, NK - 1)
                pe.wait_ge(cst_m, 1)
                for t in range(NT):
                    mm = nc.tensor.matmul(ps[:, 4, t:t + 1], xacc[:, t * P:(t + 1) * P], ones[:], start=True, stop=True)
                mm.then_inc(ss_done, 1)

            def turn_q(r, f):
                n = 2 * r + f
                pe.wait_ge(q2l_done, r + 1)
                if n:
                    pe.wait_ge(qt_done, n)
                for i in range(4):
                    mm = transpose_r(ps[:, 2, i * P:(i + 1) * P], q2[:, 4 * f + i].rearrange("p a d -> p (a d)"))
                mm.then_inc(tq_done, 1)

            def turn_k(r, f):
                n = 2 * r + f
                pe.wait_ge(k2l_done, r + 1)
                if n:
                    pe.wait_ge(ks_done, n)
                for i in range(4):
                    mm = transpose_r(ps[:, 3, i * P:(i + 1) * P], k2[:, 4 * f + i].rearrange("p a d -> p (a d)"))
                mm.then_inc(tk_done, 1)

            def scores(r, f, heads):
                n = 2 * r + f
                if 0 in heads:
                    pe.wait_ge(qt_done, n + 1)
                    pe.wait_ge(kx_done, n + 1)
                    pe.wait_ge(ks_done, n + 1)
                    if n:
                        pe.wait_ge(sd_done, n)
                    else:
                        pe.wait_ge(ms_done, 1)
                for i in heads:
                    out = ps[:, 4, i * P:(i + 1) * P]
                    nc.tensor.matmul(out, ks[:, i], qt[:, i], start=True, stop=False)
                    mm = nc.tensor.matmul(out, kx[:, i], qt[:, i], start=False, stop=True)
                if 3 in heads:
                    mm.then_inc(sc_done, 1)

            def cross(r, f, heads):
                if r == 0:
                    return
                if 0 in heads:
                    pe.wait_ge(sl_done, r)
                    if f == 0:
                        pe.wait_ge(oread, r)
                for i in heads:
                    hd = 4 * f + i
                    out = ps[:, 6, hd * HD:(hd + 1) * HD]
                    nc.tensor.matmul(out, qt[:, i], sh[:, hd], start=True, stop=False)
                    mm = nc.tensor.matmul(out, qt[:, i], sl[:, hd], start=False, stop=True)
                if 3 in heads:
                    mm.then_inc(cr_done, 1)

            def state_sum(r, hd):
                if r == NT - 1:
                    return
                if hd == 0:
                    pe.wait_ge(kdl_done, r + 1)
                    pe.wait_ge(vl_done, r + 1)
                    if r:
                        pe.wait_ge(st_done, r)
                _, mm = product(ps[:, 5, hd * HD:(hd + 1) * HD],
                                (kdh[:, hd].rearrange("p a d -> p (a d)"), kdl[:, hd].rearrange("p a d -> p (a d)")),
                                (vh[:, hd], vl[:, hd]), True, True)
                if hd == RH - 1:
                    mm.then_inc(kv_done, 1)

            def intra(r, f, i):
                if i == 0:
                    pe.wait_ge(stl_done, 2 * r + f + 1)
                    pe.wait_ge(vl_done, r + 1)
                    if f == 0 and r:
                        pe.wait_ge(oread, r)
                hd = 4 * f + i
                _, mm = product(ps[:, 7, hd * HD:(hd + 1) * HD], (sth[:, i], stl[:, i]), (vh[:, hd], vl[:, hd]), True, True)
                if i == 3:
                    mm.then_inc(in_done, 1)

            table = {m: [] for m in range(RSLOTS)}
            for f in range(2):
                for at, fn in ((4, turn_q), (5, turn_k)):
                    table[13 * f + at].append((fn, (f,)))
                for at, fn in ((9, scores), (11, cross)):
                    for i in range(2):
                        table[13 * f + at + i].append((fn, (f, (2 * i, 2 * i + 1))))
                for i in range(4):
                    table[13 * f + 15 + i].append((intra, (f, i)))
            for hd, at in enumerate((6, 7, 8, 13, 14, 19, 20, 21)):
                table[at].append((state_sum, (hd,)))
            pe.wait_ge(cst_r, 1)
            for s in range(NS):
                for k in range(NK):
                    project(s, k)
                    if s * NK + k == NK + 1:
                        sum_squares()
                    ret_slots(s, k, table)

            def transpose_f(out, in_, n=P):
                return nc.tensor.transpose(out, in_, ident_f[0:n, 0:n])

            pe.wait_ge(kraw_in, 16)
            pe.wait_ge(act_ev, act_steps(NS))
            pe.wait_ge(oread, NT)
            for i, col in enumerate((0, 3)):
                for t in range(NT):
                    mm = transpose_f(ps[:, 2 * i + t // 4, t % 4 * P:(t % 4 + 1) * P], kraw[:, t, col])
                mm.then_inc(kt_done, 1)
            for e in range(8):
                br, g_, q4 = e // 4, e // 2 % 2, e % 2
                pe.wait_ge(kl_done, 1 + br)
                if e >= 2:
                    pe.wait_ge(aks_done, e - 1)
                for i in range(4):
                    mm = transpose_r(ps[:, 4 + e % 2, i * P:(i + 1) * P],
                                     kspl[:, br, 4 * q4 + i, g_].rearrange("p a d -> p (a d)"))
                mm.then_inc(kk_done, 1)
            for i in range(2):
                pe.wait_ge(comp_in[i], 32)
                pe.wait_ge(cb_done, i + 1)
                for half in range(2):
                    for j in range(CJ):
                        mm = nc.tensor.matmul(ps[:, 6 + i, half * G * NCMP:(half + 1) * G * NCMP],
                                              cw1[:, i, j, half * P:(half + 1) * P], cb[:, i, j],
                                              start=(j == 0), stop=(j == CJ - 1))
                mm.then_inc(hid_done, 1)
            pe.wait_ge(gelu_done, 2)
            for j in range(2):
                nc.tensor.matmul(ps[0:G * NCMP, 1, 0:HD], chidT[:, 0, j], cw2[:, 0, j], start=(j == 0), stop=(j == 1))
            for g_ in range(G):
                for j in range(2):
                    mm = nc.tensor.matmul(ps[0:NCMP, 1, P + g_ * HD:P + (g_ + 1) * HD],
                                          chidT[:, 1, j, g_ * NCMP:(g_ + 1) * NCMP], cw2[:, 1, j], start=(j == 0), stop=(j == 1))
            mm.then_inc(ck_done, 1)
            pe.wait_ge(ckl_done, 1)
            nc.tensor.transpose(ps[:, 2, 0:G * NCMP].bitcast(F32R), c2[:], ident_r[0:G * NCMP, 0:G * NCMP]).then_inc(ckt_done, 1)

            pe.wait_ge(ckx_done, 1)
            pe.wait_ge(akx_done, 8)
            pe.wait_ge(akx2_done, 8)
            pe.wait_ge(kl_done, 4)

            def turn_free(st):
                n = turns_of[st] - NTR
                if n >= 0:
                    if turn_list[n][0] == "turn_q" or whole(turn_list[n]):
                        pe.wait_ge(tr_h, n + 1)
                    else:
                        pe.wait_ge(tr_l, low_of(n + 1))

            def q_turn(st):
                pe.wait_ge(aql_done, st[1] + 1)
                turn_free(st)
                for i in range(RG):
                    mm = transpose_r(ps[:, turn_bank(st), i * P:(i + 1) * P], aq2[:, i].rearrange("p a d -> p (a d)"))
                mm.then_inc(tr_full, 1)

            def qk(v, i):
                n, (t, g_), (r_, br) = 2 * RG * v + i, divmod(v, G), divmod(i, 2)
                pe.wait_ge(tr_h, turns_of["turn_q", v] + 1)
                if n >= 2:
                    pe.wait_ge(exp_done, n - 1)
                q_ = aqt[:, v % 2, r_ * P:(r_ + 1) * P]
                w0 = 0 if br == 0 else max(0, t - WIN_T)
                width = (t + 1 - w0) * P
                for c in range(0, width, 512):
                    w = min(512, width - c)
                    bank = 2 * br + c // 512
                    at = w0 * P + c
                    nc.tensor.matmul(ps[:, bank, 0:w], q_, aks[:, br, g_, at:at + w], start=True, stop=False)
                    masks = []
                    if br and t >= WIN_T and c == 0:
                        masks.append((0, far_b))
                    if c + w == width:
                        masks.append((w - P, diag_b))
                    mm = nc.tensor.matmul(ps[:, bank, 0:w], q_, akx[:, br, g_, at:at + w], start=False, stop=not masks)
                    for m, (off, mask) in enumerate(masks):
                        mm = nc.tensor.matmul(ps[:, bank, off:off + P], ident_b[:], mask, start=False, stop=(m == len(masks) - 1))
                if br:
                    sc_ = ps[:, 3, P:P + HD]
                    nc.tensor.matmul(sc_, q_, cks[:, g_ * NCMP:g_ * NCMP + HD], start=True, stop=False)
                    nc.tensor.matmul(sc_, q_, ckx[:, g_ * NCMP:g_ * NCMP + HD], start=False, stop=False)
                    mm = nc.tensor.matmul(sc_, ident_b[:], cmp_b[:, t], start=False, stop=True)
                mm.then_inc(qk_done, 1)

            def p_turn(st):
                v, j = st[1:]
                _, _, at, w = key_tiles(v)[j]
                pe.wait_ge(norm_done, 2 * RG * (v + 1))
                turn_free(st)
                for r_ in range(RG):
                    mm = transpose_f(ps[0:w, turn_bank(st), r_ * P:(r_ + 1) * P], prob[:, v % 2, r_, at:at + w])
                mm.then_inc(tr_full, 1)

            def pv(st):
                v, j = st[1:]
                tiles = key_tiles(v)
                br, kt, _, w = tiles[j]
                turn, g_ = ("turn_p", v, j), v % G
                at = place_of[turn]
                if whole(turn):
                    pe.wait_ge(tr_h, turns_of[turn] + 1)
                else:
                    pe.wait_ge(tr_l, low_of(turns_of[turn] + 1))
                if j == 0 and v:
                    pe.wait_ge(csum_done, v)
                vals = cv2[:, g_] if br == 2 else av2[:, br, kt, g_]
                out_ = ps[:, 7, :]
                first, last = j == 0, j == len(tiles) - 1
                if whole(turn):
                    mm = nc.tensor.matmul(out_, vals.bitcast(F32), ptw[0:w, at], start=first, stop=last)
                else:
                    nc.tensor.matmul(out_, vals, pth[0:w, at], start=first, stop=False)
                    mm = nc.tensor.matmul(out_, vals, ptl[0:w, at], start=False, stop=last)
                mm.then_inc(pv_done, 1)

            def ret_turn(st):
                t = st[1]
                pe.wait_ge(aro_in[t % 2], 16 * (t // 2 + 1))
                turn_free(st)
                for k in range(4):
                    mm = transpose_f(ps[:, turn_bank(st), k * P:(k + 1) * P], aro[:, t % 2, k * P:(k + 1) * P])
                mm.then_inc(tr_full, 1)

            q_turn(("turn_q", 0))
            qk(0, 0)
            for n, slot in enumerate(slots):
                for st in slot:
                    {"turn_q": q_turn, "turn_p": p_turn, "output": pv, "turn_ret": ret_turn}.get(st[0], skip)(st)
                if n + 1 < 2 * RG * NV:
                    qk(*divmod(n + 1, 2 * RG))

            pe.wait_ge(exp_done, 2 * RG * NV)
            pe.wait_ge(tr_l, low_of(len(turn_list)))
            pe.wait_ge(nsal_done, NV)
            for n in range(OPS):
                half, t = divmod(n, NT)
                tok = slice(t * P, (t + 1) * P)
                if n >= 4:
                    pe.wait_ge(op_add, n - 3)
                for k in range(NK):
                    j = half * NK + k
                    if t == 0:
                        pe.wait_ge(owl_done, j + 1)
                    hi, lo = (reth, retl) if k < 4 else (nsah, nsal)
                    first, last = product(ps[:, n % 4, :], (hi[:, k % 4, tok], lo[:, k % 4, tok]),
                                          (owh[:, j % OWR], owl[:, j % OWR]), k == 0, k == NK - 1)
                    if (n == NT - 1 and k > 0) or (n == NT and k == 0):
                        first.then_inc(ow_used, 1)
                last.then_inc(op_done, 1)
            for e in range(2 * NT):
                t, q = divmod(e, 2)
                pe.wait_ge(hs_done, t + 1)
                if e >= 4:
                    pe.wait_ge(ht_l, e - 3)
                else:
                    pe.wait_ge(csum_done, NV)
                for i in range(4):
                    k = 4 * q + i
                    mm = transpose_f(ps[:, 4 + e % 4, i * P:(i + 1) * P], hs[:, t, k * P:(k + 1) * P])
                mm.then_inc(ht_full, 1)

            def up(f, u, part, between=None):
                for k in range(NK):
                    if part == 0 and k % 4 == 0:
                        pe.wait_ge(wul_done, 2 * f + k // 4 + 1)
                    cols = slice(part * P, (part + 1) * P)
                    wh_, wl_ = wuh[:, u, k, cols], wul[:, u, k, cols]
                    for i, (w_, x_) in enumerate(((wh_, hth), (wh_, htl), (wl_, hth))):
                        for half in range(2):
                            mm = nc.tensor.matmul(ps[:, 2 * part + half, :], w_, x_[:, k, half * 512:(half + 1) * 512],
                                                  start=(k == 0 and i == 0), stop=(k == NK - 1 and i == 2))
                    if k == NK - 1:
                        mm.then_inc(up_v if part else up_g, 1)
                    if between is not None:
                        between(2 * k)
                        between(2 * k + 1)

            def down(f, u, o_, first):
                t, half = divmod(o_, 2)
                if o_ == 0:
                    pe.wait_ge(ffl_done, f)
                    pe.wait_ge(wdl_done, f)
                if not first or o_ >= 4:
                    pe.wait_ge(dn_add, OPS * f - OPS + o_ - 3)
                _, mm = product(ps[:, 4 + o_ % 4, :], (ffh[:, u, t * P:(t + 1) * P], ffl[:, u, t * P:(t + 1) * P]),
                                (wdh[:, u, half * CH:(half + 1) * CH], wdl[:, u, half * CH:(half + 1) * CH]), True, True)
                mm.then_inc(dn_done, 1)

            def ffn_pe(f, u, first):
                if first != 0:
                    pe.wait_ge(gate_ev, f)
                up(f, u, 0)
                if first != 0:
                    pe.wait_ge(ffa_done, f)
                    up(f, u, 1, lambda o_: down(f, 1 - u, o_, first == 1))
                else:
                    up(f, u, 1)

            pe.wait_ge(ht_l, 2 * NT)
            ffn_pe(0, 0, 0)
            ffn_pe(1, 1, 1)
            with pe.Fori(0, NF // 2 - 1) as i:
                ffn_pe(2 * i + 2, 0, None)
                ffn_pe(2 * i + 3, 1, None)
            for o_ in range(OPS):
                down(NF, 1, o_, False)

            def gt_turn(t):
                for q in range(2):
                    e = 2 * t + q
                    if e >= 4:
                        pe.wait_ge(gt_l, e - 3)
                    for i in range(4):
                        k = 4 * q + i
                        mm = transpose_f(ps[:, 4 + e % 4, i * P:(i + 1) * P], h[:, t, k * P:(k + 1) * P])
                    mm.then_inc(gt_full, 1)

            pe.wait_ge(dn_add, OPS * NF)
            gt_turn(0)
            pe.wait_ge(gwl_done, 4 * NP_)
            for n in range(OPS):
                half, t = divmod(n, NT)
                if n + 1 < NT:
                    gt_turn(n + 1)
                if n >= 2:
                    pe.wait_ge(pmul_done, n - 1)
                for k in range(NP_):
                    product(ps[:, 2 + n % 2, :], (peh[:, k, t // 4, t % 4 * P:(t % 4 + 1) * P], pel[:, k, t // 4, t % 4 * P:(t % 4 + 1) * P]),
                            (pwh[:, k, half], pwl[:, k, half]), k == 0, k == NP_ - 1)
                if half == 0:
                    pe.wait_ge(gt_l, 2 * t + 2)
                tok = slice(t * P, (t + 1) * P)
                for k in range(NK):
                    j = half * NK + k
                    if t == 0:
                        pe.wait_ge(gwl_done, 4 * NP_ + j + 1)
                    first, last = product(ps[:, n % 2, :], (hth[:, k, tok], htl[:, k, tok]),
                                          (gwh[:, j % GWR], gwl[:, j % GWR]), k == 0, k == NK - 1)
                    if (n == NT - 1 and k > 0) or (n == NT and k == 0):
                        first.then_inc(gw_used, 1)
                last.then_inc(pg_done, 1)

        @block.vector
        def _(dve):
            count = [0]

            def chain(ins):
                count[0] += 1
                ins.then_inc(dve_chain, 1)
                dve.wait_ge(dve_chain, count[0])

            def mark(ins):
                count[0] += 1
                ins.then_inc(dve_chain, 1)
                return count[0]

            dve.wait_ge(cst_in, 48)
            chain(nc.vector.memset(ones[:], 1.0))
            nc.vector.tensor_copy(ident_b[:], ident_f).then_inc(cst_m, 1)
            nc.vector.tensor_copy(masks_b[:], cst[:, C_DIAG:C_DT]).then_inc(cst_m, 1)

            def split_w(j):
                dve.wait_ge(wh_done, j + 1)
                n = CW[j // NK]
                nc.vector.tensor_tensor(wl[:, j % RW, 0:n], wraw[:, j % RR, 0:n],
                                        wh[:, j % RW, 0:n].bitcast(F32), ALU.subtract).then_inc(wl_done, 1)

            chain(nc.vector.tensor_copy(posf[:], posi[:]))
            chain(nc.vector.tensor_tensor(ang[:], bc(posf[:].rearrange("p (t o) -> p t o", o=1), [P, NT, NA]),
                                          bc(cst[:, C_INV:C_INV + NA].rearrange("p (o a) -> p o a", o=1), [P, NT, NA]),
                                          ALU.mult))
            chain(nc.vector.tensor_scalar(turns[:], ang[:], 1.0 / (2 * np.pi), MAGIC, ALU.mult, ALU.add))
            chain(nc.vector.tensor_scalar(turns[:], turns[:], -MAGIC, None, ALU.add))
            for part in two_pi_parts():
                chain(nc.vector.scalar_tensor_tensor(ang[:], turns[:], -part, ang[:], ALU.mult, ALU.add))
            nc.vector.tensor_scalar(red[:], ang[:], PI_IN, -PI_IN, ALU.min, ALU.max).then_inc(red_done, 1)
            dve.wait_ge(red_done, 1)
            chain(nc.vector.scalar_tensor_tensor(red2[:], red[:], -1.0, red[:], ALU.mult, ALU.max))
            nc.vector.tensor_scalar(red2[:], red2[:], -1.0, np.pi / 2, ALU.mult, ALU.add).then_inc(red_done, 1)

            for k in range(NK):
                dve.wait_ge(xh_done, k + 1)
                nc.vector.scalar_tensor_tensor(xtl[:, k], xraw[:, k % XR], wmix[:, k:k + 1], xth[:, k].bitcast(F32),
                                               ALU.mult, ALU.subtract).then_inc(xl_done, 1)
                split_w(k)
            dve.wait_ge(ss_done, 1)
            nc.vector.tensor_scalar(ms[:], ps[:, 4, 0:NT], 1.0 / D, EPS, ALU.mult, ALU.add).then_inc(ms_done, 1)
            dve.wait_ge(rstd_done, 1)
            dve.wait_ge(sin_done, 2)
            for i in range(2):
                chain(nc.vector.tensor_tensor(tab[:, i], tab[:, i], bc(rstd[:].rearrange("p (t o) -> p t o", o=1), [P, NT, NA]),
                                              ALU.mult))
            chain(nc.vector.tensor_scalar(tab[:, 2:4], tab[:, 0:2], SCALE, None, ALU.mult))

            def rope(s, src, dst, heads, half, cs):
                cos, sin = cs
                shape = [P, heads, half]
                n = heads * 2 * half
                wide = lambda t: bc(t.rearrange("p (o a) -> p o a", o=1), shape)
                A = ropa[:, 0:n].rearrange("p (a b c) -> p a b c", b=2, c=half)
                B = ropb[:, 0:n].rearrange("p (a b c) -> p a b c", b=2, c=half)
                x1, x2 = src[:, :, 0:half], src[:, :, half:2 * half]
                nc.vector.tensor_tensor(A[:, :, 0], x1, wide(cos), ALU.mult)
                nc.vector.tensor_tensor(A[:, :, 1], x2, wide(cos), ALU.mult)
                nc.vector.tensor_tensor(B[:, :, 0], x2, wide(sin), ALU.mult)
                nc.vector.tensor_tensor(B[:, :, 1], x1, wide(sin), ALU.mult).then_inc(dve_rd, 1)
                dve.wait_ge(dve_rd, dve_steps(s + 1))
                nc.vector.tensor_tensor(dst[:, :, 0:half], A[:, :, 0], B[:, :, 0], ALU.subtract)
                nc.vector.tensor_tensor(dst[:, :, half:2 * half], A[:, :, 1], B[:, :, 1], ALU.add).then_inc(dve_st, 1)

            def evac(s):
                c, t = divmod(s, NT)
                if c not in DVE_CH:
                    return
                dve.wait_ge(pj_done, s + 1)
                if dve_steps(s):
                    dve.wait_ge(dve_st, dve_steps(s))
                if s >= NST:
                    stored(dve, s - NST)
                src, dst = ps[:, s % 2, :], stage[:, s % NST, :]
                if c < 2:
                    v = lambda ap: ap.rearrange("p (a d) -> p a d", d=HD)
                    rope(s, v(src), v(dst), RH, ROPE_R, (tab[:, 2 * c, t, 0:ROPE_R], tab[:, 2 * c + 1, t, 0:ROPE_R]))
                else:
                    dve.wait_ge(copy_ev, copy_steps(s + 1))
                    n = QH if c == 4 else 6
                    v = lambda ap: ap[:, 0:n * HD].rearrange("p (a d) -> p a d", d=HD)
                    rope(s, v(src), v(dst), n, ROPE_N, (tab[:, 0, t, ROPE_R:NA], tab[:, 1, t, ROPE_R:NA]))

            def heads(i):
                return rin[:, i].rearrange("p (a d) -> p a d", a=RH)

            def per_head(at, n=HD):
                return bc(cst[:, at:at + RH].rearrange("p (a o) -> p a o", o=1), [P, RH, n])

            def q_low(r):
                dve.wait_ge(q2h_done, r + 1)
                nc.vector.tensor_tensor(q2[:, :, 1], heads(0), q2[:, :, 0].bitcast(F32), ALU.subtract).then_inc(q2l_done, 1)

            def k_low(r):
                dve.wait_ge(k2h_done, r + 1)
                nc.vector.tensor_tensor(k2[:, :, 1], heads(1), k2[:, :, 0].bitcast(F32), ALU.subtract).then_inc(k2l_done, 1)

            def v_low(r):
                dve.wait_ge(vh_done, r + 1)
                nc.vector.tensor_tensor(vl[:], heads(2), vh[:].bitcast(F32), ALU.subtract).then_inc(vl_done, 1)

            def k_decay(r):
                dve.wait_ge(rin_s[1], 16 * (r + 1))
                if r:
                    dve.wait_ge(kdl_done, r)
                nc.vector.tensor_tensor(kd[:], heads(1), per_head(C_KD), ALU.mult).then_inc(kd_done, 1)

            def kd_low(r):
                if r == NT - 1:
                    return
                dve.wait_ge(kdh_done, r + 1)
                nc.vector.tensor_tensor(kdl[:], bc(kd[:].rearrange("p a (o d) -> p a o d", o=1), [P, RH, 2, HD]),
                                        kdh[:].bitcast(F32), ALU.subtract).then_inc(kdl_done, 1)

            def ks_copy(r, f):
                n = 2 * r + f
                dve.wait_ge(tk_done, n + 1)
                if n:
                    dve.wait_ge(sc_done, n)
                nc.vector.tensor_copy(ks[:].rearrange("p a d -> p (a d)"), ps[:, 3, :]).then_inc(ks_done, 1)

            def decay(r, f):
                n = 2 * r + f
                dve.wait_ge(sc_done, n + 1)
                if n:
                    dve.wait_ge(stl_done, n)
                nc.vector.tensor_tensor(sd[:].rearrange("p a d -> p (a d)"), ps[:, 4, :],
                                        cst[:, C_DT + 4 * f * P:C_DT + 4 * (f + 1) * P], ALU.mult).then_inc(sd_done, 1)

            def st_low(r, f):
                n = 2 * r + f
                dve.wait_ge(sth_done, n + 1)
                nc.vector.tensor_tensor(stl[:], sd[:], sth[:].bitcast(F32), ALU.subtract).then_inc(stl_done, 1)

            def state(r):
                if r == NT - 1:
                    return
                dve.wait_ge(kv_done, r + 1)
                kv = ps[:, 5, :].rearrange("p (a d) -> p a d", a=RH)
                if r == 0:
                    nc.vector.tensor_copy(stf[:], kv).then_inc(st_done, 1)
                else:
                    dve.wait_ge(sl_done, r)
                    chain(nc.vector.tensor_tensor(stt[:], stf[:], per_head(C_CD), ALU.mult))
                    nc.vector.tensor_tensor(stf[:], stt[:], kv, ALU.add).then_inc(st_done, 1)

            def state_low(r):
                if r == NT - 1:
                    return
                dve.wait_ge(sh_done, r + 1)
                nc.vector.tensor_tensor(sl[:], stf[:], sh[:].bitcast(F32), ALU.subtract).then_inc(sl_done, 1)

            def o_read(r):
                dve.wait_ge(in_done, 2 * r + 2)
                intra = ps[:, 7, :].rearrange("p (a d) -> p a d", a=RH)
                if r:
                    dve.wait_ge(oout_done, r)
                    dve.wait_ge(cr_done, 2 * r)
                    chain(nc.vector.tensor_tensor(osq[:], ps[:, 6, :].rearrange("p (a d) -> p a d", a=RH),
                                                  per_head(C_QD), ALU.mult))
                    nc.vector.tensor_tensor(oc[:], osq[:], intra, ALU.add).then_inc(oread, 1)
                else:
                    nc.vector.tensor_copy(oc[:], intra).then_inc(oread, 1)

            def o_center(r):
                dve.wait_ge(oread, r + 1)
                chain(nc.vector.reduce_sum(gst[:, 0], oc[:], AX_X))
                chain(nc.vector.tensor_scalar(gst[:, 1], gst[:, 0], 1.0 / HD, None, ALU.mult))
                nc.vector.tensor_tensor(oc[:], oc[:], bc(gst[:, 1].rearrange("p (a o) -> p a o", o=1), [P, RH, HD]),
                                        ALU.subtract).then_inc(osub_done, 1)

            def o_var(r):
                dve.wait_ge(osq_done, r + 1)
                chain(nc.vector.reduce_sum(gst[:, 0], osq[:], AX_X))
                nc.vector.tensor_scalar(gst[:, 2], gst[:, 0], 1.0 / HD, EPS, ALU.mult, ALU.add).then_inc(var_done, 1)

            def o_out(r):
                dve.wait_ge(orstd_done, r + 1)
                dve.wait_ge(rin_s[3], 16 * (r + 1))
                if r:
                    dve.wait_ge(reto_s, 16 * r)
                chain(nc.vector.tensor_tensor(oc[:], oc[:], bc(gst[:, 3].rearrange("p (a o) -> p a o", o=1), [P, RH, HD]),
                                              ALU.mult))
                chain(nc.vector.tensor_tensor(oc[:], oc[:], gnb[:].rearrange("p (a d) -> p a d", a=RH), ALU.mult))
                nc.vector.tensor_tensor(oout[:], oc[:], heads(3), ALU.mult).then_inc(oout_done, 1)

            dve.wait_ge(cst_in, 64)
            table = {0: [(k_decay, ())], 1: [(q_low, ())], 2: [(k_low, ())], 3: [(v_low, ())], 4: [(kd_low, ())],
                     6: [(ks_copy, (0,))], 11: [(decay, (0,))], 13: [(st_low, (0,))],
                     19: [(ks_copy, (1,))], 23: [(state, ()), (decay, (1,))], 25: [(st_low, (1,))], 27: [(state_low, ())],
                     33: [(o_read, ())], 40: [(o_center, ())], 42: [(o_var, ())], 46: [(o_out, ())]}
            for s in range(NS + 1):
                for k in range(NK):
                    if k == 0 and s >= 1:
                        evac(s - 1)
                    if s < NS and (j := slice_at(s, k)) is not None:
                        split_w(j)
                    ret_slots(s, k, table)

            def low(out_, full, high):
                return nc.vector.tensor_tensor(out_, full, high.bitcast(F32), ALU.subtract)

            dve.wait_ge(kraw_in, 16)
            gd = lambda ap: ap.rearrange("p t (g d) -> p t g d", g=G)
            for i in range(2):
                dve.wait_ge(kh_done, i + 1)
                low(kspl[:, i, :, :, 1], gd(kraw[:, :, 1 + i]), kspl[:, i, :, :, 0]).then_inc(kl_done, 1)
            dve.wait_ge(cpos_in, 16)
            for i in range(2):
                dve.wait_ge(kt_done, i + 1)
                for g_ in range(G):
                    src = ps[g_ * HD:(g_ + 1) * HD, 2 * i:2 * i + 2, :].rearrange("p a (m b c) -> p (a m) b c", b=8, c=2)
                    for par in range(2):
                        for q in range(2):
                            half = slice(par * HD, (par + 1) * HD)
                            ins = nc.vector.tensor_tensor(
                                cb[half, i, q * 8:(q + 1) * 8, g_ * NCMP:(g_ + 1) * NCMP],
                                src[:, q:q + NCMP, :, par].rearrange("p m b -> p b m"),
                                bc(cposb[half, q * 8:(q + 1) * 8].rearrange("p (b o) -> p b o", o=1), [HD, 8, NCMP]), ALU.add)
                ins.then_inc(cb_done, 1)
            for e in range(8):
                br, g_, q4 = e // 4, e // 2 % 2, e % 2
                dve.wait_ge(aks_done, e + 1)
                nc.vector.tensor_copy(akx[0:HD, br, g_, q4 * 512:(q4 + 1) * 512],
                                      aks[HD:P, br, g_, q4 * 512:(q4 + 1) * 512].bitcast(F32)).then_inc(akx2_done, 1)
            for i in range(2):
                dve.wait_ge(kh_done, 3 + i)
                low(av2[:, i, :, :, HD:], gd(vraw[:, :, i]), av2[:, i, :, :, 0:HD]).then_inc(kl_done, 1)
            dve.wait_ge(ckh_done, 1)
            low(c2[:, HD:], ps[0:G * NCMP, 1, 0:HD], c2[:, 0:HD])
            low(cv2[:, :, HD:], ps[0:NCMP, 1, P:2 * P].rearrange("p (g d) -> p g d", g=G), cv2[:, :, 0:HD]).then_inc(ckl_done, 1)
            dve.wait_ge(ckt_done, 1)
            nc.vector.memset(cks[:, G * NCMP:].bitcast(F32), 0.0)
            nc.vector.tensor_copy(cks[:, 0:G * NCMP], ps[:, 2, 0:G * NCMP]).then_inc(cks_done, 1)

            def q_split_low(st):
                v = st[1]
                dve.wait_ge(aqh_done, v + 1)
                low(aq2[:, :, 1], aqr[:, v % 2].rearrange("p (r d) -> p r d", r=RG), aq2[:, :, 0]).then_inc(aql_done, 1)

            def row_max(v, i):
                n, t, br = 2 * RG * v + i, v // G, i % 2
                dve.wait_ge(qk_done, n + 1)
                m = n % 4
                s_ = ps[:, 2 * br:2 * br + 2, :].rearrange("p a n -> p (a n)")
                if br == 0:
                    return mark(nc.vector.reduce_max(mx[:, m, 0:1], s_[:, 0:(t + 1) * P], AX_X))
                w = (t - max(0, t - WIN_T) + 1) * P
                nc.vector.reduce_max(mx[:, m, 0:1], s_[:, 0:w], AX_X)
                return mark(nc.vector.reduce_max(mx[:, m, 1:2], s_[:, 5 * P:5 * P + NCMP], AX_X))

            def exp_bias(v, i, maxima):
                m, w = (2 * RG * v + i) % 4, 1 + i % 2
                dve.wait_ge(dve_chain, maxima)
                nc.vector.tensor_scalar(nb[:, m, 0:w], mx[:, m, 0:w], FLOOR, -SCALE, ALU.max, ALU.mult).then_inc(nb_done, 1)

            def guard_sum(v, i):
                n, w = 2 * RG * v + i, 1 + i % 2
                dve.wait_ge(exp_done, n + 1)
                return mark(nc.vector.tensor_scalar(rd[:, n % 4, 0:w], den[:, n % 4, 0:w], 1e-30, None, ALU.max))

            def invert_sum(v, i, guarded):
                m, w = (2 * RG * v + i) % 4, 1 + i % 2
                dve.wait_ge(dve_chain, guarded)
                return mark(nc.vector.reciprocal(rd2[:, m, 0:w], rd[:, m, 0:w]))

            def normalize(v, i, inverted):
                n, (t, g_), (r_, br) = 2 * RG * v + i, divmod(v, G), divmod(i, 2)
                m, hd = n % 4, g_ * RG + r_
                dve.wait_ge(dve_chain, inverted)
                pr = prob[:, v % 2, r_]
                if br == 0:
                    p_ = pr[:, 0:(t + 1) * P]
                    nc.vector.tensor_scalar(p_, p_, rd2[:, m, 0:1], gates[:, t, hd, 1:2], ALU.mult, ALU.mult).then_inc(norm_done, 1)
                else:
                    width = (t - max(0, t - WIN_T) + 1) * P
                    p_ = pr[:, S:S + width]
                    nc.vector.tensor_scalar(p_, p_, rd2[:, m, 0:1], gates[:, t, hd, 2:3], ALU.mult, ALU.mult)
                    at = S + (WIN_T + 1) * P
                    p_ = pr[:, at:at + NCMP]
                    nc.vector.tensor_scalar(p_, p_, rd2[:, m, 1:2], gates[:, t, hd, 0:1], ALU.mult, ALU.mult).then_inc(norm_done, 1)

            def p_low(st):
                at = place_of[st]
                w = key_tiles(st[1])[st[2]][3]
                dve.wait_ge(tr_h, turns_of[st] + 1)
                low(ptl[0:w, at], ps[0:w, turn_bank(st), :], pth[0:w, at]).then_inc(tr_l, 1)

            def ret_low(st):
                t = st[1]
                dve.wait_ge(tr_h, turns_of[st] + 1)
                tok = slice(t * P, (t + 1) * P)
                low(retl[:, :, tok], ps[:, turn_bank(st), :].rearrange("p (k n) -> p k n", k=4), reth[:, :, tok]).then_inc(tr_l, 1)

            def add_parts(st):
                v = st[1]
                dve.wait_ge(swap_done, v + 1)
                if v:
                    dve.wait_ge(nsal_done, v)
                o_ = ps[:, 7, :].rearrange("p (a b n) -> p a b n", a=2, b=2)
                c_ = comb[:].rearrange("p c (a n) -> p c a n", a=2)
                nc.vector.tensor_tensor(c_[0:HD, 1], o_[0:HD, :, 0], c_[0:HD, 0], ALU.add)
                nc.vector.tensor_tensor(c_[HD:P, 1], o_[HD:P, :, 1], c_[HD:P, 0], ALU.add).then_inc(csum_done, 1)

            def nsa_low(st):
                v = st[1]
                t, g_ = divmod(v, G)
                c_ = comb[:].rearrange("p c (a n) -> p c a n", a=2)
                dve.wait_ge(nsah_done, v + 1)
                tok = slice(t * P, (t + 1) * P)
                low(nsal[:, 2 * g_:2 * g_ + 2, tok], c_[:, 1], nsah[:, 2 * g_:2 * g_ + 2, tok]).then_inc(nsal_done, 1)

            q_split_low(("split_q", 0))
            for n, slot in enumerate(slots):
                lows = [st for st in slot if st[0] in ("turn_p", "turn_ret") and not whole(st)]
                if n < 2 * RG * NV:
                    maxima = row_max(*divmod(n, 2 * RG))
                if 0 < n <= 2 * RG * NV:
                    guarded = guard_sum(*divmod(n - 1, 2 * RG))
                if n < 2 * RG * NV:
                    exp_bias(*divmod(n, 2 * RG), maxima)
                if 0 < n <= 2 * RG * NV:
                    inverted = invert_sum(*divmod(n - 1, 2 * RG), guarded)
                for st in lows:
                    {"turn_p": p_low, "turn_ret": ret_low}[st[0]](st)
                if 0 < n <= 2 * RG * NV:
                    normalize(*divmod(n - 1, 2 * RG), inverted)
                for st in slot:
                    {"split_q": q_split_low, "sum": add_parts, "combine": nsa_low}.get(st[0], skip)(st)

            def ow_low(j):
                dve.wait_ge(owh_done, j + 1)
                low(owl[:, j % OWR], owraw[:, j % RR], owh[:, j % OWR]).then_inc(owl_done, 1)

            def stream_ms(t):
                dve.wait_ge(hsq_done, t + 1)
                nc.vector.tensor_scalar(hst[:, 1, t:t + 1], hst[:, 0, t:t + 1], 1.0 / D, EPS, ALU.mult, ALU.add).then_inc(hms_done, 1)

            def stream_norm(t):
                dve.wait_ge(hrs_done, t + 1)
                nc.vector.scalar_tensor_tensor(hs[:, t], h[:, t], hst[:, 2, t:t + 1], wfb[:], ALU.mult, ALU.mult).then_inc(hs_done, 1)

            for j in range(OWR):
                ow_low(j)
            dve.wait_ge(h_in, 16)
            for n in range(OPS + 2):
                half, t = divmod(n, NT)
                if n < OPS:
                    for k in range(NK):
                        if (j := late_slice(n, k, OWR)) is not None:
                            ow_low(j)
                    dve.wait_ge(op_done, n + 1)
                    hh = h[:, t, half * CH:(half + 1) * CH]
                    nc.vector.tensor_tensor(hh, hh, ps[:, n % 4, :], ALU.add).then_inc(op_add, 1)
                if n == NT:
                    dve.wait_ge(wfb_in, 16)
                if 0 <= n - NT - 1 < NT:
                    stream_ms(n - NT - 1)
                if 0 <= n - NT - 2 < NT:
                    stream_norm(n - NT - 2)
            for e in range(2 * NT):
                t, q = divmod(e, 2)
                dve.wait_ge(ht_h, e + 1)
                tok = slice(t * P, (t + 1) * P)
                low(htl[:, 4 * q:4 * q + 4, tok], ps[:, 4 + e % 4, :].rearrange("p (k n) -> p k n", k=4),
                    hth[:, 4 * q:4 * q + 4, tok]).then_inc(ht_l, 1)

            def wu_low(f, u):
                for i in range(2):
                    dve.wait_ge(wuh_done, 2 * f + i + 1)
                    low(wul[:, u, i * 4:i * 4 + 4], wuraw[:, i], wuh[:, u, i * 4:i * 4 + 4]).then_inc(wul_done, 1)

            def wd_low(f, u):
                dve.wait_ge(wdh_done, f + 1)
                low(wdl[:, u], wdraw[:], wdh[:, u]).then_inc(wdl_done, 1)

            def down_add(f, o_):
                t, half = divmod(o_, 2)
                dve.wait_ge(dn_done, OPS * f - OPS + o_ + 1)
                hh = h[:, t, half * CH:(half + 1) * CH]
                nc.vector.tensor_tensor(hh, hh, ps[:, 4 + o_ % 4, :], ALU.add).then_inc(dn_add, 1)

            def ffn_dve(f, u, q, first, last=False):
                if not last:
                    wu_low(f + 1, 1 - u)
                dve.wait_ge(tap_done, f + 1)
                nc.vector.scalar_tensor_tensor(act_[:], gate[:, 1:S + 1], taps[:, u, 1:2], act_[:], ALU.mult, ALU.add).then_inc(conv_mid, 1)
                dve.wait_ge(conv_mid, f + 1)
                nc.vector.scalar_tensor_tensor(act_[:], gate[:, 0:S], taps[:, u, 0:1], act_[:], ALU.mult, ALU.add).then_inc(conv_done, 1)
                if first != 0:
                    for o_ in range(OPS):
                        down_add(f, o_)
                dve.wait_ge(up_v, f + 1)
                dve.wait_ge(silu_done, f + 1)
                if first != 0:
                    dve.wait_ge(ffl_done, f)
                nc.vector.tensor_tensor(ffa[:], act_[:], ps[:, 2:4, :].rearrange("p a n -> p (a n)"), ALU.mult).then_inc(ffa_done, 1)
                dve.wait_ge(ffh_done, f + 1)
                low(ffl[:, u], ffa[:], ffh[:, u]).then_inc(ffl_done, 1)
                if not last:
                    wd_low(f + 1, 1 - u)

            chain(nc.vector.memset(gate[:, 0:2], 0.0))
            wu_low(0, 0)
            wd_low(0, 0)
            ffn_dve(0, 0, 0, 0)
            ffn_dve(1, 1, 0, 1)
            with dve.Fori(0, NF // 2 - 2) as i:
                ffn_dve(2 * i + 2, 0, i + 1, None)
                ffn_dve(2 * i + 3, 1, i + 1, None)
            ffn_dve(NF - 2, 0, NF // 2 - 1, None)
            ffn_dve(NF - 1, 1, NF // 2 - 1, None, last=True)
            for o_ in range(OPS):
                down_add(NF, o_)

            def gw_low(j):
                dve.wait_ge(gwh_done, j + 1)
                low(part_of(j, pel, pwl, gwl), gwraw[:, j // 2 % RR, j % 2], part_of(j, peh, pwh, gwh)).then_inc(gwl_done, 1)

            def gt_low(e):
                t, q = divmod(e, 2)
                dve.wait_ge(gt_h, e + 1)
                tok = slice(t * P, (t + 1) * P)
                low(htl[:, 4 * q:4 * q + 4, tok], ps[:, 4 + e % 4, :].rearrange("p (k n) -> p k n", k=4),
                    hth[:, 4 * q:4 * q + 4, tok]).then_inc(gt_l, 1)

            def final_ms(t):
                dve.wait_ge(fsq_done, t + 1)
                nc.vector.tensor_scalar(fst[:, 1, t:t + 1], fst[:, 0, t:t + 1], 1.0 / D, EPS, ALU.mult, ALU.add).then_inc(fms_done, 1)

            def final_norm(t):
                dve.wait_ge(frs_done, t + 1)
                nc.vector.scalar_tensor_tensor(ost[:, t % 2], h[:, t], fst[:, 2, t:t + 1], fwb[:], ALU.mult, ALU.mult).then_inc(fin_done, 1)

            for j in range(4 * NP_ + GWR):
                gw_low(j)
                if j in (1, 3):
                    gt_low(j // 2)
            for n in range(OPS + 3):
                half, t = divmod(n, NT)
                if 0 < n < NT:
                    gt_low(2 * n)
                    gt_low(2 * n + 1)
                for k in range(NK):
                    if (j := late_slice(n, k, GWR)) is not None:
                        gw_low(4 * NP_ + j)
                if n < OPS:
                    dve.wait_ge(sig_done, n + 1)
                    if n >= 2:
                        dve.wait_ge(pg_add, n - 1)
                    nc.vector.tensor_tensor(pmul[:, n % 2], sig[:, n % 2], ps[:, 2 + n % 2, :], ALU.mult).then_inc(pmul_done, 1)
                    dve.wait_ge(pmul_done, n + 1)
                    hh = h[:, t, half * CH:(half + 1) * CH]
                    nc.vector.tensor_tensor(hh, hh, pmul[:, n % 2], ALU.add).then_inc(pg_add, 1)
                if n == NT:
                    dve.wait_ge(wfb_in, 32)
                if 0 <= n - NT - 2 < NT:
                    final_ms(n - NT - 2)
                if 0 <= n - NT - 3 < NT:
                    final_norm(n - NT - 3)



def laid_out(i):
    c = np.ascontiguousarray
    f = {n: np.asarray(v) for n, v in i.items()}
    x = f["x"][0]
    w = f["w_in"][0]
    o = 4 * RH * HD
    kv = lambda n: w[:, o + QH * HD + n * G * HD:o + QH * HD + (n + 1) * G * HD]
    cols = [w[:, n * CH:(n + 1) * CH] for n in range(5)]
    cols.append(np.concatenate([kv(0), kv(2), kv(4), kv(1)], 1))
    cols.append(np.concatenate([kv(3), kv(5), w[:, o + QH * HD + 6 * G * HD:], np.zeros((D, CH - CW[6]), np.float32)], 1))
    w_in = np.concatenate([m.reshape(NK, P, CH).transpose(1, 0, 2).reshape(P, NK * CH) for m in cols], 1)
    cols = lambda v: c(v.reshape(-1, P).T)
    up = f["ffn_w_up"][0].reshape(NK, P, 2, NF, P).transpose(3, 1, 0, 2, 4).reshape(NF, P, NK * 2 * P)
    conv = np.stack([*f["ffn_conv_w"][0], f["ffn_conv_b"][0]], -1).reshape(NF, P, 4)
    return dict(
        xt=c(x.T), x=c(x), pt=c(f["p"][0, 0].T), pos=c(f["positions"][0].astype(np.int32).reshape(NT, P).T),
        cst_d=constants(), wmix_d=cols(f["norm_mix_w"][0]), wffn_d=c(f["norm_ffn_w"][0]), gnw=c(f["ret_gn_w"][0]),
        w_in=c(w_in), cpos=c(f["cmp_pos"][0].reshape(CJ, P).T), ck_w1=c(f["cmp_k_w1"][0]), ck_w2=c(f["cmp_k_w2"][0]),
        cv_w1=c(f["cmp_v_w1"][0]), cv_w2=c(f["cmp_v_w2"][0]), w_out=c(f["w_out"][0]), w_up=c(up), conv_d=c(conv),
        w_down=c(f["ffn_w_down"][0].reshape(NF, P, D)), ple_w=c(f["ple_w"][0]), ple_gw=c(f["ple_gate_w"][0]), fnw=c(f["final_norm_w"]))


def kernel(**inputs):
    import concourse.bacc as bacc
    from concourse.bass_utils import run_bass_kernel_spmd

    nc = bacc.Bacc("TRN2", target_bir_lowering=False, num_devices=1)
    arrays, args = {}, {}
    for name, a in laid_out(inputs).items():
        arrays["in_" + name] = a
        args[name] = nc.dram_tensor("in_" + name, a.shape, mybir.dt.from_np(a.dtype), kind="ExternalInput").ap()
    out = nc.dram_tensor("out", [S, D], F32, kind="ExternalOutput").ap()
    build(nc, **args, out=out)
    r = run_bass_kernel_spmd(nc, [arrays], core_ids=[0])
    return r.results[0]["out"].reshape(1, S, D)
```
